# Optimizing a Trainium2 kernel written in Bass

```python
import math
import jax, jax.numpy as jnp
from jax import lax
import numpy as np

D_MODEL = 1024
BATCH = 1
SEQ = 256
DEPTH = 2

GRID_W = 64
CTX_LEN = 256
N_EVEN = (DEPTH + 1) // 2
N_ODD = DEPTH // 2
N_MOD = 6
EPS = 1e-6

HY_C = D_MODEL // 2
HY_ORDER = 2
HY_EMB = 33
HY_BANDS = (HY_EMB - 1) // 2
HY_FILT_W = 64
HY_SHORT = 3
HY_DECAY_SHORT_PCT = 0.3
HY_DECAY_LONG_PCT = 1.5
HY_TARGET = 1e-2
HEAD_DIM = 64
N_Q_HEADS = (D_MODEL // 2) // HEAD_DIM
N_KV_HEADS = N_Q_HEADS // 4
GQA_GROUP = N_Q_HEADS // N_KV_HEADS
WINDOW = 128
ATTN_BLK = 128
ROPE_BASE = 10000.0
AB_IN = 3 * HY_C + (N_Q_HEADS + 2 * N_KV_HEADS) * HEAD_DIM
AB_OUT = HY_C + N_Q_HEADS * HEAD_DIM

HG_HEADS = 8
HG_DK = D_MODEL // HG_HEADS
HG_DV = D_MODEL // HG_HEADS
HG_F = HG_HEADS * HG_DK
HG_IN = 3 * HG_F + 2 * HG_HEADS * HG_DV
HG_CHUNK = 64

PEER_HEADS = 8
PEER_TOPK = 16
N_KEYS = 128
N_EXPERTS = N_KEYS * N_KEYS
PEER_QDIM = 256
PEER_TOK_BLK = 128

kernel_name = "hybrid_hyena_swa_hgrn2_peer_dit"

F32 = jnp.float32

def rmsnorm(x, g):
    x32 = x.astype(F32)
    y = x32 * lax.rsqrt(jnp.mean(x32 * x32, axis=-1, keepdims=True) + EPS)
    return y.astype(x.dtype) * g

def modulate(x, shift, scale):
    return x * (1 + scale) + shift

def axial_rope_cos_sin(L):
    rows = L // GRID_W
    r = jnp.broadcast_to(jnp.arange(rows)[:, None], (rows, GRID_W)).reshape(-1).astype(F32)
    col = jnp.broadcast_to(jnp.arange(GRID_W)[None, :], (rows, GRID_W)).reshape(-1).astype(F32)
    nf = HEAD_DIM // 4
    inv = ROPE_BASE ** (-jnp.arange(nf, dtype=F32) / nf)
    ang = jnp.concatenate([r[:, None] * inv, col[:, None] * inv], axis=-1)
    return jnp.cos(ang), jnp.sin(ang)

def apply_rope(x, cos, sin):
    shp = x.shape
    nf = HEAD_DIM // 4
    xa = x.reshape(shp[:-1] + (2, 2, nf))
    bshape = (1, shp[1]) + (1,) * (x.ndim - 3) + (2, nf)
    c = cos.reshape(bshape).astype(x.dtype)
    s = sin.reshape(bshape).astype(x.dtype)
    a, b = xa[..., 0, :], xa[..., 1, :]
    out = jnp.stack([a * c - b * s, b * c + a * s], axis=-2)
    return out.reshape(shp)

def hyena_filters(L, w1, b1, w2, b2, w3, freq):
    t = jnp.linspace(0.0, 1.0, L, dtype=F32)[:, None]
    w = 2.0 * math.pi * jnp.arange(L, dtype=F32)[:, None] / L
    f = jnp.linspace(1e-4, HY_BANDS - 1, HY_BANDS, dtype=F32)[None, :]
    z = jnp.concatenate([t, jnp.cos(f * w), -jnp.sin(f * w)], axis=-1)
    fr = freq.astype(F32)
    hdn = jnp.sin(fr * (z @ w1.astype(F32) + b1.astype(F32)))
    hdn = jnp.sin(fr * (hdn @ w2.astype(F32) + b2.astype(F32)))
    h = (hdn @ w3.astype(F32)).reshape(L, HY_ORDER, 2, HY_C)
    max_decay = math.log(HY_TARGET) / HY_DECAY_SHORT_PCT
    min_decay = math.log(HY_TARGET) / HY_DECAY_LONG_PCT
    deltas = jnp.abs(jnp.linspace(min_decay, max_decay, HY_C, dtype=F32))
    h = h * jnp.exp(-t * deltas)[:, None, None, :]
    return h / jnp.sum(jnp.abs(h), axis=(0, 2), keepdims=True)

def hyena_mixer(u, conv_w, conv_b, w1, b1, w2, b2, w3, freq, d_skip):
    L = u.shape[1]
    up = jnp.pad(u, ((0, 0), (1, 1), (0, 0)))
    u = up[:, :-2] * conv_w[0] + up[:, 1:-1] * conv_w[1] + up[:, 2:] * conv_w[2] + conv_b
    v, x1, x2 = jnp.split(u, 3, axis=-1)
    h = hyena_filters(L, w1, b1, w2, b2, w3, freq)
    two_sided = jnp.concatenate([h[:, :, 0], jnp.zeros((1, HY_ORDER, HY_C), F32), h[:0:-1, :, 1]], axis=0)
    hf = jnp.fft.rfft(two_sided, axis=0)
    z = v
    for n, gate in enumerate((x1, x2)):
        zf = jnp.fft.rfft(z.astype(F32), n=2 * L, axis=1)
        conv = jnp.fft.irfft(zf * hf[None, :, n, :], n=2 * L, axis=1)[:, :L]
        z = gate * (conv.astype(z.dtype) + d_skip[n] * z)
    return z

def window_attention(q, k, v, kc, vc, sink):
    B, L = q.shape[:2]
    nb = L // ATTN_BLK
    scale = HEAD_DIM ** -0.5
    qb = q.reshape(B, nb, ATTN_BLK, N_KV_HEADS, GQA_GROUP, HEAD_DIM)

    def band(t):
        tp = jnp.pad(t, ((0, 0), (ATTN_BLK, ATTN_BLK), (0, 0), (0, 0)))
        tp = tp.reshape(B, nb + 2, ATTN_BLK, N_KV_HEADS, HEAD_DIM)
        return jnp.concatenate([tp[:, :-2], tp[:, 1:-1], tp[:, 2:]], axis=2)

    kw, vw = band(k), band(v)
    s_win = jnp.einsum('bnqhgd,bnkhd->bnhgqk', qb, kw).astype(F32) * scale
    qpos = jnp.arange(nb)[:, None, None] * ATTN_BLK + jnp.arange(ATTN_BLK)[None, :, None]
    kpos = jnp.arange(nb)[:, None, None] * ATTN_BLK - ATTN_BLK + jnp.arange(3 * ATTN_BLK)[None, None, :]
    valid = (kpos >= 0) & (kpos < L) & (jnp.abs(qpos - kpos) <= WINDOW)
    s_win = jnp.where(valid[None, :, None, None], s_win, -jnp.inf)
    s_ctx = jnp.einsum('bnqhgd,bchd->bnhgqc', qb, kc).astype(F32) * scale
    s_sink = jnp.broadcast_to(sink.astype(F32)[None, None, :, :, None, None], s_win.shape[:-1] + (1,))
    p = jax.nn.softmax(jnp.concatenate([s_sink, s_win, s_ctx], axis=-1), axis=-1).astype(q.dtype)
    nw = 3 * ATTN_BLK
    o = (jnp.einsum('bnhgqk,bnkhd->bnqhgd', p[..., 1:1 + nw], vw)
         + jnp.einsum('bnhgqc,bchd->bnqhgd', p[..., 1 + nw:], vc))
    return o.reshape(B, L, N_Q_HEADS * HEAD_DIM)

def context_attention(qc, kc, vc, sink):
    B, Lc = qc.shape[:2]
    s = jnp.einsum('bqhgd,bkhd->bhgqk', qc, kc).astype(F32) * (HEAD_DIM ** -0.5)
    s_sink = jnp.broadcast_to(sink.astype(F32)[None, :, :, None, None], s.shape[:-1] + (1,))
    p = jax.nn.softmax(jnp.concatenate([s_sink, s], axis=-1), axis=-1).astype(qc.dtype)
    o = jnp.einsum('bhgqk,bkhd->bqhgd', p[..., 1:], vc)
    return o.reshape(B, Lc, N_Q_HEADS * HEAD_DIM)

def hyena_attention_mixer(a_lat, a_ctx, w_in, w_out, conv_w, conv_b, fw1, fb1, fw2, fb2, fw3, ffreq,
                          d_skip, sink, need_ctx):
    B, L, _ = a_lat.shape
    o_q = 3 * HY_C
    o_k = o_q + N_Q_HEADS * HEAD_DIM
    o_v = o_k + N_KV_HEADS * HEAD_DIM

    def split(p):
        Lx = p.shape[1]
        q = p[..., o_q:o_k].reshape(B, Lx, N_KV_HEADS, GQA_GROUP, HEAD_DIM)
        k = p[..., o_k:o_v].reshape(B, Lx, N_KV_HEADS, HEAD_DIM)
        v = p[..., o_v:].reshape(B, Lx, N_KV_HEADS, HEAD_DIM)
        return p[..., :o_q], q, k, v

    hy_l, q_l, k_l, v_l = split(a_lat @ w_in)
    hy_c, q_c, k_c, v_c = split(a_ctx @ w_in)
    cos, sin = axial_rope_cos_sin(L)
    q_l = apply_rope(q_l, cos, sin)
    k_l = apply_rope(k_l, cos, sin)
    sink = sink.reshape(N_KV_HEADS, GQA_GROUP)
    hy_p = (conv_w, conv_b, fw1, fb1, fw2, fb2, fw3, ffreq, d_skip)
    y_lat = jnp.concatenate([hyena_mixer(hy_l, *hy_p),
                             window_attention(q_l, k_l, v_l, k_c, v_c, sink)], axis=-1) @ w_out
    y_ctx = None
    if need_ctx:
        y_ctx = jnp.concatenate([hyena_mixer(hy_c, *hy_p),
                                 context_attention(q_c, k_c, v_c, sink)], axis=-1) @ w_out
    return y_lat, y_ctx

def gla_chunk_scan(q, k, v, logf, S0):
    B, H, L, dk = q.shape
    dv = v.shape[-1]
    nc = L // HG_CHUNK
    tri = jnp.tril(jnp.ones((HG_CHUNK, HG_CHUNK), dtype=bool))

    def to_chunks(t):
        return jnp.moveaxis(t.reshape(B, H, nc, HG_CHUNK, t.shape[-1]), 2, 0)

    def step(S, inp):
        qc, kc, vc, gc = inp
        b = jnp.cumsum(gc, axis=2)
        o_inter = jnp.einsum('bhtk,bhkv->bhtv', qc * jnp.exp(b), S)
        diff = jnp.where(tri[:, :, None], b[:, :, :, None, :] - b[:, :, None, :, :], -jnp.inf)
        A = jnp.einsum('bhtk,bhtsk,bhsk->bhts', qc, jnp.exp(diff), kc)
        o = o_inter + jnp.einsum('bhts,bhsv->bhtv', A, vc)
        b_last = b[:, :, -1:, :]
        S = jnp.exp(b_last[:, :, 0, :, None]) * S + jnp.einsum('bhsk,bhsv->bhkv', kc * jnp.exp(b_last - b), vc)
        return S, o

    S, o = lax.scan(step, S0, (to_chunks(q), to_chunks(k), to_chunks(v), to_chunks(logf)))
    return S, jnp.moveaxis(o, 0, 2).reshape(B, H, L, dv)

def hgrn2_mixer(a_lat, a_ctx, w_in, w_out, lb, onorm_g, need_ctx):
    def proj(a):
        p = (a @ w_in).astype(F32)
        B, Lx, _ = p.shape
        q, f_f, f_b, i, g = jnp.split(p, [HG_F, 2 * HG_F, 3 * HG_F, 3 * HG_F + HG_HEADS * HG_DV], axis=-1)

        def heads(t, d):
            return t.reshape(B, Lx, HG_HEADS, d).transpose(0, 2, 1, 3)

        def gates(f, lbd):
            fg = lbd + (1.0 - lbd) * jax.nn.sigmoid(f)
            return heads(1.0 - fg, HG_DK), heads(jnp.log(fg), HG_DK)

        return heads(jax.nn.silu(q), HG_DK), heads(i, HG_DV), g, gates(f_f, lb[0]), gates(f_b, lb[1])

    def flip(t):
        return t[:, :, ::-1]

    def readout(o, g, like):
        B, H, Lx, _ = o.shape
        o = rmsnorm(o.transpose(0, 2, 1, 3), onorm_g.astype(F32)).reshape(B, Lx, H * HG_DV)
        return (o * jax.nn.silu(g)).astype(like.dtype) @ w_out

    B = a_lat.shape[0]
    S0 = jnp.zeros((B, HG_HEADS, HG_DK, HG_DV), F32)
    qc, ic, gc, (kcf, lcf), (kcb, lcb) = proj(a_ctx)
    S_cf, o_cf = gla_chunk_scan(qc, kcf, ic, lcf, S0)
    S_cb, o_cb = gla_chunk_scan(flip(qc), flip(kcb), flip(ic), flip(lcb), S0)
    ql, il, gl, (klf, llf), (klb, llb) = proj(a_lat)
    _, o_lf = gla_chunk_scan(ql, klf, il, llf, S_cf)
    _, o_lb = gla_chunk_scan(flip(ql), flip(klb), flip(il), flip(llb), S_cb)
    y_lat = readout(o_lf + flip(o_lb), gl, a_lat)
    y_ctx = readout(o_cf + flip(o_cb), gc, a_ctx) if need_ctx else None
    return y_lat, y_ctx

def peer_ffn(x, wq, keys, U, V):
    B, L, D = x.shape
    K = PEER_TOPK
    q = (x @ wq).reshape(B, L, PEER_HEADS, 2, PEER_QDIM // 2)
    s = jnp.einsum('blhpd,hpnd->blhpn', q, keys).astype(F32)
    s1, i1 = lax.top_k(s[..., 0, :], K)
    s2, i2 = lax.top_k(s[..., 1, :], K)
    cand = (s1[..., :, None] + s2[..., None, :]).reshape(B, L, PEER_HEADS, K * K)
    top_s, top_j = lax.top_k(cand, K)
    e1 = jnp.take_along_axis(i1, top_j // K, axis=-1)
    e2 = jnp.take_along_axis(i2, top_j % K, axis=-1)
    idx = e1 * N_KEYS + e2
    gate = jax.nn.softmax(top_s, axis=-1).astype(x.dtype)
    nblk = (B * L) // PEER_TOK_BLK
    xb = x.reshape(nblk, PEER_TOK_BLK, D)
    ib = idx.reshape(nblk, PEER_TOK_BLK, PEER_HEADS * K)
    gb = gate.reshape(nblk, PEER_TOK_BLK, PEER_HEADS * K)

    def block(args):
        xt, it, gt = args
        act = jax.nn.gelu(jnp.einsum('tkd,td->tk', U[it], xt), approximate=False) * gt
        return jnp.einsum('tk,tkd->td', act, V[it])

    return lax.map(block, (xb, ib, gb)).reshape(B, L, D)

def setup_inputs(seed: int = 0) -> dict:
    key = jax.random.key(seed)
    ks = iter(jax.random.split(key, 40))
    D = D_MODEL

    def nrm(shape, s):
        return jax.random.normal(next(ks), shape, F32) * s

    return {
        "x": nrm((BATCH, SEQ, D), 1.0),
        "c": nrm((BATCH, D), 1.0),
        "ctx": nrm((BATCH, CTX_LEN, D), 1.0),
        "c_ctx": nrm((D,), 1.0),
        "ada_w": nrm((DEPTH, D, N_MOD * D), 0.5 * D ** -0.5),
        "ada_b": nrm((DEPTH, N_MOD * D), 0.01),
        "norm1_g": 1.0 + nrm((DEPTH, D), 0.05),
        "norm2_g": 1.0 + nrm((DEPTH, D), 0.05),
        "final_g": 1.0 + nrm((D,), 0.05),
        "ab_w_in": nrm((N_EVEN, D, AB_IN), D ** -0.5),
        "ab_w_out": nrm((N_EVEN, AB_OUT, D), AB_OUT ** -0.5),
        "hy_conv_w": nrm((N_EVEN, HY_SHORT, 3 * HY_C), HY_SHORT ** -0.5),
        "hy_conv_b": nrm((N_EVEN, 3 * HY_C), 0.01),
        "hy_filt_w1": nrm((N_EVEN, HY_EMB, HY_FILT_W), HY_EMB ** -0.5),
        "hy_filt_b1": nrm((N_EVEN, HY_FILT_W), 0.02),
        "hy_filt_w2": nrm((N_EVEN, HY_FILT_W, HY_FILT_W), HY_FILT_W ** -0.5),
        "hy_filt_b2": nrm((N_EVEN, HY_FILT_W), 0.02),
        "hy_filt_w3": nrm((N_EVEN, HY_FILT_W, HY_ORDER * 2 * HY_C), HY_FILT_W ** -0.5),
        "hy_filt_freq": 1.0 + nrm((N_EVEN, HY_FILT_W), 0.1),
        "hy_skip": nrm((N_EVEN, HY_ORDER, HY_C), 0.5),
        "attn_sink": nrm((N_EVEN, N_Q_HEADS), 0.5),
        "hg_w_in": nrm((N_ODD, D, HG_IN), D ** -0.5),
        "hg_w_out": nrm((N_ODD, HG_HEADS * HG_DV, D), (HG_HEADS * HG_DV) ** -0.5),
        "hg_lb_logits": nrm((DEPTH, 2, HG_F), 0.5),
        "hg_onorm_g": 1.0 + nrm((N_ODD, HG_DV), 0.05),
        "peer_wq": nrm((DEPTH, D, PEER_HEADS * PEER_QDIM), D ** -0.5),
        "peer_keys": nrm((DEPTH, PEER_HEADS, 2, N_KEYS, PEER_QDIM // 2), (PEER_QDIM // 2) ** -0.5),
        "peer_u": nrm((DEPTH, N_EXPERTS, D), D ** -0.5),
        "peer_v": nrm((DEPTH, N_EXPERTS, D), 1.0),
    }

def reference(x, c, ctx, c_ctx, ada_w, ada_b, norm1_g, norm2_g, final_g, ab_w_in, ab_w_out,
              hy_conv_w, hy_conv_b, hy_filt_w1, hy_filt_b1, hy_filt_w2, hy_filt_b2, hy_filt_w3,
              hy_filt_freq, hy_skip, attn_sink, hg_w_in, hg_w_out, hg_lb_logits, hg_onorm_g,
              peer_wq, peer_keys, peer_u, peer_v):
    lb_p = jax.nn.softmax(hg_lb_logits.astype(F32), axis=0)
    lb_all = jnp.cumsum(lb_p, axis=0) - lb_p[0:1]
    h_lat, h_ctx = x, ctx
    for l in range(DEPTH):
        need_ctx = l < DEPTH - 1
        mod_l = (jax.nn.silu(c) @ ada_w[l] + ada_b[l])[:, None, :]
        mod_c = jax.nn.silu(c_ctx) @ ada_w[l] + ada_b[l]
        sh1, sc1, g1, sh2, sc2, g2 = jnp.split(mod_l, N_MOD, axis=-1)
        sh1c, sc1c, g1c, sh2c, sc2c, g2c = jnp.split(mod_c, N_MOD, axis=-1)
        a_lat = modulate(rmsnorm(h_lat, norm1_g[l]), sh1, sc1)
        a_ctx = modulate(rmsnorm(h_ctx, norm1_g[l]), sh1c, sc1c)
        j = l // 2
        if l % 2 == 0:
            y_lat, y_ctx = hyena_attention_mixer(
                a_lat, a_ctx, ab_w_in[j], ab_w_out[j], hy_conv_w[j], hy_conv_b[j],
                hy_filt_w1[j], hy_filt_b1[j], hy_filt_w2[j], hy_filt_b2[j], hy_filt_w3[j],
                hy_filt_freq[j], hy_skip[j], attn_sink[j], need_ctx)
        else:
            y_lat, y_ctx = hgrn2_mixer(a_lat, a_ctx, hg_w_in[j], hg_w_out[j], lb_all[l].astype(a_lat.dtype),
                                       hg_onorm_g[j], need_ctx)
        h_lat = h_lat + g1 * y_lat
        h_lat = h_lat + g2 * peer_ffn(modulate(rmsnorm(h_lat, norm2_g[l]), sh2, sc2),
                                      peer_wq[l], peer_keys[l], peer_u[l], peer_v[l])
        if need_ctx:
            h_ctx = h_ctx + g1c * y_ctx
            h_ctx = h_ctx + g2c * peer_ffn(modulate(rmsnorm(h_ctx, norm2_g[l]), sh2c, sc2c),
                                           peer_wq[l], peer_keys[l], peer_u[l], peer_v[l])
    return rmsnorm(h_lat, final_g)


_drawn_inputs = setup_inputs


def setup_inputs(seed=0):
    import zlib

    import numpy as np

    out = dict(_drawn_inputs(seed))
    spreads = {}
    factors = {'hy_conv_b': 13.608,
     'hy_filt_b1': 4.916,
     'hy_filt_b2': 4.25,
     'hy_filt_freq': 3.779,
     'attn_sink': 8.0,
     'hg_lb_logits': 3.53,
     'hg_onorm_g': 2.983}
    for name, (base, spread) in spreads.items():
        noise = np.random.default_rng([zlib.crc32(name.encode()), seed]).standard_normal(out[name].shape)
        drawn = base * np.exp(spread * noise) if base else spread * noise
        out[name] = __import__('jax').numpy.asarray(drawn.astype(out[name].dtype))
    for name, factor in factors.items():
        out[name] = (out[name] * factor).astype(out[name].dtype)
    return out
```

```python
from contextlib import ExitStack

import numpy as np

import concourse.bass as bass
from concourse import mybir

F32 = mybir.dt.float32
F32R = mybir.dt.float32r
U32 = mybir.dt.uint32
ALU = mybir.AluOpType
ACT = mybir.ActivationFunctionType
AXX = mybir.AxisListType.X

P = 128
D = 1024
KD = D // P
SEQ = 256
T = 2 * SEQ
TT = T // P
NMOD = 6
EPS = 1e-6
HYC = 512
HC = HYC // P
NQ = 8
HD = 64
NH = 8
TOPK = 16
NKEY = 128
CHUNKS = SEQ // P
LEVELS = 7
RING = 4
TURN = 8
TILE = KD * P
NEG = -3.0e38
ARENA = 33792
TWO_PI = 2.0 * np.pi
PI_A = 6.28125
PI_B = float(np.float32(TWO_PI - PI_A) // np.float32(2.0 ** -20) * 2.0 ** -20)
PI_C = float(np.float32(TWO_PI - PI_A - PI_B))
ROUND = 12582912.0

N_ADA = 2 * NMOD * KD
ADA_FIRST = 2 * KD
ADA_AB = 2
ADA_ROUTE = (N_ADA - ADA_FIRST - 16 * ADA_AB) // TT
N_ABIN, N_OUT, N_WQ, N_HGIN, N_PEER = 18, KD, 16, 40, 2 * NKEY
AT_ADA = 0
AT_ABIN = AT_ADA + ADA_FIRST
AT_ABOUT = AT_ABIN + N_ABIN + 16 * ADA_AB
AT_WQ0 = AT_ABOUT + N_OUT
AT_ROUTE = AT_WQ0 + N_WQ
AT_PEER = [AT_ROUTE + TT * ADA_ROUTE, AT_ROUTE + TT * ADA_ROUTE + N_PEER, 0]
AT_HGIN = AT_PEER[1] + N_PEER
AT_HGOUT = AT_HGIN + N_HGIN
AT_WQ1 = AT_HGOUT + N_OUT
AT_PEER[2] = AT_WQ1 + N_WQ


def at_abin(j):
    return AT_ABIN + j + ADA_AB * min(j, 16)


def at_wq(l, j):
    return (AT_WQ0, AT_WQ1)[l] + j


ADA_GROUPS = ([(4 * g, 4, AT_ADA + 4 * g) for g in range(ADA_FIRST // 4)]
              + [(ADA_FIRST + ADA_AB * j, ADA_AB, at_abin(j) + 1) for j in range(16)]
              + [(ADA_FIRST + 16 * ADA_AB + ADA_ROUTE * j, ADA_ROUTE, AT_ROUTE + ADA_ROUTE * j) for j in range(TT)])
ROUTE_STEPS = 19

QKEYS = 32
GTOK = 8
GROUPS = SEQ // GTOK
QUARTERS = NKEY // QKEYS
PASS_GROUP = [GROUPS, 5 * GROUPS, 9 * GROUPS]
PASS_TOK = [0, SEQ, 0]


def tile_u(m):
    return 2 * m - 1 if m else 0


def tile_v(m):
    return min(2 * m + 2, N_PEER - 1)


def wait(eng, sem, value):
    if isinstance(value, int) and value <= 0:
        return
    eng.wait_ge(sem, value)


class Chain:

    def __init__(self, eng, sem, settle):
        self.settle = settle
        self.eng, self.sem, self.n, self.i, self.per = eng, sem, 0, None, 0

    def at(self, n):
        return n if self.i is None else self.i * self.per + n

    def done(self, ins):
        self.n += 1
        ins.then_inc(self.sem, 1)
        self.eng.wait_ge(self.sem, self.at(self.n))
        if self.i is not None:
            self.settle()

    def enter(self, i, per):
        self.i, self.per = i, per

    def leave(self, trips, n0):
        assert self.n - n0 == self.per, (self.n - n0, self.per)
        self.n = n0 + trips * self.per
        self.i = None


def build(nc, a, out):
    with ExitStack() as ctx:
        def sb(name, words, dt=F32):
            return ctx.enter_context(nc.sbuf_tensor(name, [P, words], dt))

        def sem(name):
            return ctx.enter_context(nc.semaphore(name))

        arena_at = -(-nc.sbuf_base // 32) * 32
        arena = sb("arena", ARENA)
        h_t = sb("h_t", KD * T)
        a_t = sb("a_t", KD * T)
        wring = sb("wring", RING * TILE)
        hand = sb("hand", 1024)
        slots = sb("slots", 3 * T)
        gate_parts = sb("gate_parts", 2 * T)
        ident = sb("ident", P)
        ones = sb("ones", P)
        iota = sb("iota", P)
        mods = sb("mods", 2 * NMOD * KD * 2)
        gmod = sb("gmod", 4 * KD * 2)
        gains = sb("gains", 5 * KD)
        csil = sb("csil", KD * 2)
        adab = sb("adab", 2 * NMOD * KD)
        conv = sb("conv", 4 * 12)
        dskip = sb("dskip", 2 * HC)
        sinks = sb("sinks", 2 * NQ)
        lbs = sb("lbs", 8 * 16)
        ong = sb("ong", 1)
        filt = sb("filt", 4)
        small = sb("small", 16)
        tick = sb("tick", 1)
        ps = ctx.enter_context(nc.psum_tensor("ps", [P, 8, 512], F32))

        H = h_t[:, :].rearrange("p (k t) -> p k t", k=KD)
        A = a_t[:, :].rearrange("p (k t) -> p k t", k=KD)
        W = wring[:, :].rearrange("p (r k n) -> p r k n", r=RING, k=KD)
        M = mods[:, :].rearrange("p (l s c z) -> p l s c z", l=2, s=NMOD, c=KD)
        M2 = mods[:, :].rearrange("p (m z) -> p m z", z=2)
        GM = gmod[:, :].rearrange("p (n c z) -> p n c z", n=4, c=KD)
        GN = gains[:, :].rearrange("p (n c) -> p n c", n=5)
        CS = csil[:, :].rearrange("p (k z) -> p k z", z=2)
        rstd = hand[:, 0:T]
        GP = gate_parts[:, :].rearrange("p (t q) -> p t q", q=2)
        SL = slots[:, :].rearrange("p (q t) -> p q t", q=3)

        def over(name, at, words):
            return nc.alloc_sbuf_tensor_at(name, [P, words], F32R, offset=arena_at + 4 * at)

        def view(at, pattern=None, **kw):
            n = 1
            for v in kw.values():
                n *= v
            x = arena[:, at:at + n]
            return x.rearrange(pattern, **kw) if pattern else x

        COSF = view(0, "p (c f) -> p c f", c=2, f=256)
        SINF = view(512, "p (c f) -> p c f", c=2, f=256)
        COSG = view(1024, "p (c t) -> p c t", c=2, t=256)
        SING = view(1536, "p (c t) -> p c t", c=2, t=256)
        HF = view(2048, "p (o q f c) -> p o q f c", o=2, q=2, f=2, c=512)
        HRAW = view(6144, "p (t o d c) -> p t o d c", t=2, o=2, d=2, c=512)
        HABS = view(10240, "p (t o d c) -> p t o d c", t=2, o=2, d=2, c=512)
        HSUM = view(14336, "p (o t c) -> p o t c", o=2, t=2, c=512)
        HDIF = view(16384, "p (o t c) -> p o t c", o=2, t=2, c=512)
        RNRM = view(18432, "p (o c) -> p o c", o=2, c=512)
        FW3 = arena[0:64, 19456:21504]
        ZPOS = arena[0:33, 21504:21760]
        FARG = arena[0:64, 21760:22016]
        FRND = arena[0:64, 22016:22272]
        FHID = [arena[0:64, 22272:22528], arena[0:64, 22528:22784]]
        DECAY = view(22784, "p (t c) -> p t c", t=2, c=512)
        FW1 = arena[0:33, 23808:23872]
        FW2 = arena[0:64, 23872:23936]
        U = view(6144, "p (j t) -> p j t", j=12, t=T)
        UC = view(12288, "p (j t) -> p j t", j=12, t=T)
        ZT = view(18432, "p (t c) -> p t c", t=TT, c=512)
        PF = view(20480, "p (s q f c) -> p s q f c", s=2, q=2, f=2, c=512)
        QT = view(24576, "p (j t) -> p j t", j=4, t=T)
        KT = arena[:, 26624:27136]
        VT = view(27136, "p (t n) -> p t n", t=TT, n=P)
        Z1 = view(27648, "p (c t) -> p c t", c=HC, t=T)
        AMASK = view(29696, "p (i k) -> p i k", i=2, k=512)
        ROPE = view(30720, "p (q t) -> p q t", q=2, t=SEQ)
        ROT = arena[:, 31232:31360]
        RTMP = arena[:, 31360:31872]
        MIX = U
        SQ = view(24576, "p (k t) -> p k t", k=KD, t=T)
        ASC = view(18432, "p (b n) -> p b n", b=2, n=512)
        APR = view(19456, "p (b n) -> p b n", b=2, n=512)
        APT = view(20480, "p (b k q) -> p b k q", b=2, k=4, q=P)
        CVT = view(29696 - 2048, "p (c t) -> p c t", c=4, t=T)

        PQT = view(0, "p (j t) -> p j t", j=16, t=T)
        KEYS = view(8192, "p (j n) -> p j n", j=16, n=NKEY)
        PQC = view(10240, "p (j t) -> p j t", j=16, t=P)
        PS1 = view(12288, "p (j n) -> p j n", j=16, n=NKEY)
        PS2 = view(14336, "p (j n) -> p j n", j=16, n=NKEY)
        CAND = view(16384, "p (h n) -> p h n", h=NH, n=256)
        CAN2 = view(18432, "p (h n) -> p h n", h=NH, n=256)
        EQ = view(20480, "p (h k m) -> p h k m", h=NH, k=TOPK, m=TOPK)
        TV = view(22528, "p (j k) -> p j k", j=16, k=TOPK)
        TIU = view(22784, "p (j k) -> p j k", j=16, k=TOPK).bitcast(U32)
        TIF = view(23040, "p (j k) -> p j k", j=16, k=TOPK)
        SV = view(23296, "p (h k) -> p h k", h=NH, k=TOPK)
        SJU = view(23424, "p (h k) -> p h k", h=NH, k=TOPK).bitcast(U32)
        HIU = view(23552, "p (q h k) -> p q h k", q=2, h=NH, k=TOPK).bitcast(U32)
        HIF = view(23808, "p (q h k) -> p q h k", q=2, h=NH, k=TOPK)
        GATE = view(24064, "p (q h k) -> p q h k", q=3, h=NH, k=TOPK)
        GSUM = view(24448, "p (q h) -> p q h", q=2, h=NH)
        G = view(0, "p (b e t) -> p b e t", b=2, e=QKEYS, t=SEQ)
        WHI, WLO = [over(n, at, 4 * TILE)[:, :].rearrange("p (r k n) -> p r k n", r=4, k=KD)
                    for n, at in (("w_hi", 16384), ("w_lo", 20480))]
        XHI, XLO = [over(n, at, KD * SEQ)[:, :].rearrange("p (k t) -> p k t", k=KD)
                    for n, at in (("x_hi", 24576), ("x_lo", 26624))]
        OHB = over("second_onehot", 28672, 2 * GTOK * P)[:, :].rearrange("p (g u e) -> p g u e", g=2, u=GTOK)
        OHA = over("first_onehot", 30720, 4 * GTOK * QKEYS)[:, :]\
            .rearrange("p (g u q e) -> p g u q e", g=2, u=GTOK, q=2)
        EQK = view(31744, "p (g u e) -> p g u e", g=2, u=GTOK, e=QKEYS)
        GRND = over("gate_rounded", 28672, T)
        GL = view(32256, "p (r t) -> p r t", r=2, t=SEQ)
        ACH, ACL = [over(n, at, 2 * SEQ)[:, :].rearrange("p (r t) -> p r t", r=2)
                    for n, at in (("act_hi", 32768), ("act_lo", 33280))]
        I16 = iota[:, 0:TOPK]

        RQ = view(0, "p (h t) -> p h t", h=NH, t=SEQ)
        RG = view(2048, "p (h t) -> p h t", h=NH, t=SEQ)
        RKL = view(4096, "p (d h t) -> p d h t", d=2, h=NH, t=SEQ)
        RKC = view(8192, "p (d h t) -> p d h t", d=2, h=NH, t=SEQ)
        LF = view(12288, "p (m t) -> p m t", m=16, t=T)
        IV = view(20480, "p (t h n) -> p t h n", t=TT, h=NH, n=P)
        EL = view(24576, "p (d m t) -> p d m t", d=2, m=16, t=129)
        EC = view(28704, "p (d h t) -> p d h t", d=2, h=NH, t=SEQ)
        CK = view(12288, "p (d h t) -> p d h t", d=2, h=NH, t=SEQ)
        CKT = view(16384, "p (t d h n) -> p t d h n", t=2, d=2, h=NH, n=P)
        LK = view(12288, "p (d h t) -> p d h t", d=2, h=NH, t=P)
        LKT = view(14336, "p (d h n) -> p d h n", d=2, h=NH, n=P)
        ST = a_t[:, 0:4096].rearrange("p (z d h n) -> p z d h n", z=2, d=2, h=NH)
        QI = view(8192, "p (d h t) -> p d h t", d=2, h=NH, t=SEQ)
        LV = [[view(12288 + 4096 * b + 2048 * q, "p (m t) -> p m t", m=16, t=P) for q in range(2)] for b in range(2)]
        AT_ = view(28704, "p (m t) -> p m t", m=16, t=P)
        masks = view(30752, "p (l t) -> p l t", l=8, t=P).bitcast(U32)
        MX1 = view(30752, "p (h t) -> p h t", h=NH, t=SEQ)
        OSQ = view(12288, "p (h t) -> p h t", h=NH, t=SEQ)
        ORS = view(14336, "p (h t) -> p h t", h=NH, t=SEQ)

        names = """consts_in arena_in keys_in masks_in x_in out_done w_used
            tables_ready c_ready ada_taken mods_ready
            f_proj f_arg f_sin f_raw f_rawtaken f_abs f_norm f_rnorm f_parts f_spec f_spectaken f_done
            sq_ready norm_summed ms_ready std_ready hn_ready a_ready
            ab_ready ab_taken cv_mid cv_done
            zt_ready zt_taken zf_ready pf_ready yt_ready z_ready 
            rot_ready rope_done
            sc_ready sc_taken nmax_ready exp_ready pn_ready pt_ready pt_taken pv_done att_done
            h_ready dec_in dec_exp
            wq_ready wq_taken qc_ready route_scores scores_in scores_ready scores_used diff_ready gate_exp gates_ready
            slots_t slots_in
            eq_ready oh_ready oh_used g_high g_taken
            xhi_ready x_ready hi_ready part_used gelu_done mul_ready acthi_ready act_ready
            hg_ready hg_taken sig_ready fk_done ln_done scan_done
            ck_exp ck_ready ck_t ck_in cs_ready cs_taken
            lk_exp lk_ready lk_t lk_in ls_ready ls_done
            qi_exp qi_ready lv_diff lv_exp lv_ready lv_prod lv_taken
            oi_ready osq_ready ors_ready oms_ready ostd_ready mx_ready
            f_in dve_step lb_diff lb_exp""".split()
        S = {n: sem(n) for n in names}
        w_loaded = [sem(f"w_loaded{r}") for r in range(RING)]
        block = ctx.enter_context(nc.Block())

        def settle_dve():
            nc.vector.tensor_copy(tick[:, 0:1], ones[:, 0:1])

        def gate_sums(n):
            return ps[:, 2 + n % 2, :].rearrange("p (t q e) -> p q e t", t=GTOK, q=2)

        def landed(eng, n, i=0):
            eng.wait_ge(w_loaded[n % RING], i * (16 * TURN // RING) + 16 * (n // RING + 1))

        def quarters(eng, turn, ready=lambda q: None):
            for q in range(QUARTERS):
                ready(q)
                e0, first_turn, last_turn = q * QKEYS, int(q == 0), QKEYS // 4 - int(q == QUARTERS - 1)
                if first_turn:
                    turn(q, 0, 0)
                with eng.Fori(first_turn, last_turn) as i:
                    turn(q, i, e0)
            turn(QUARTERS - 1, 0, NKEY - 4)

        first = [(csil[:, :], a["cc"]), (ident[:, :], a["ident"]), (ones[:, :], a["ones"]), (iota[:, :], a["iota"]),
                 (adab[:, :], a["adab"]), (gains[:, :], a["gains"]), (conv[:, :], a["conv"]),
                 (dskip[:, :], a["dskip"]), (sinks[:, 0:NQ], a["sink"]), (lbs[:, 0:32], a["lbl"]),
                 (ong[:, :], a["ong"])]
        filters_in = [(ZPOS, a["zpos"]), (FW1, a["fw1"]), (filt[0:64, 0:3], a["fvec"]), (FW2, a["fw2"]),
                      (FW3, a["fw3"]), (arena[:, 22784:23808], a["decay"]), (arena[:, 0:2048], a["dft"])]
        arena_loads = [(arena[:, 29696:30720], a["amask"]), (arena[:, 30720:31360], a["rope"])]

        @block.sync
        def _(sp):
            sp.dma_start(h_t[:, :], a["xT"]).then_inc(S["x_in"], 16)

            def load(n, src, i=0):
                wait(sp, S["w_used"], i * TURN + (n - RING + 1))
                sp.dma_start(wring[:, n % RING * TILE:(n % RING + 1) * TILE], src).then_inc(w_loaded[n % RING], 16)

            def row(src, x):
                return src[bass.ds(x, 1), :, :].rearrange("a p n -> p (a n)") if not isinstance(x, int) else src[x]

            def stream(n0, src, count, r0=0):
                turns = count // TURN
                for j in range(TURN):
                    load(n0 + j, row(src, r0 + j))
                if turns > 1:
                    with sp.Fori(1, turns) as i:
                        for j in range(TURN):
                            load(n0 + j, row(src, i * TURN + (r0 + j)), i)
                for j in range(turns * TURN, count):
                    load(n0 + j, row(src, r0 + j))

            def stream_with(at, src, count, groups):
                for j in range(count):
                    load(at(j), src[j])
                    if j < len(groups):
                        m, k, pos = groups[j]
                        for x in range(k):
                            load(pos + x, a["ada"][m + x])

            def experts(n0, u, v):
                def pairs(i, js):
                    for j in js:
                        load(n0 + 1 + 2 * j, row(u, i * 4 + (j + 1)), i)
                        load(n0 + 2 + 2 * j, row(v, i * 4 + j), i)

                load(n0, row(u, 0))
                pairs(0, range(4))
                with sp.Fori(1, NKEY // 4 - 1) as i:
                    pairs(i, range(4))
                last = NKEY - 4
                for e in range(last, NKEY):
                    if e + 1 < NKEY:
                        load(n0 + 1 + 2 * e, u[e + 1])
                    load(n0 + (2 + 2 * e if e + 1 < NKEY else 1 + 2 * e), v[e])

            stream(AT_ADA, a["ada"], ADA_FIRST)
            stream_with(at_abin, a["abin"], N_ABIN, ADA_GROUPS[4:20])
            stream(AT_ABOUT, a["about"], N_OUT)
            stream(AT_WQ0, a["wq0"], N_WQ)
            stream(AT_ROUTE, a["ada"], TT * ADA_ROUTE, ADA_FIRST + 16 * ADA_AB)
            experts(AT_PEER[0], a["u0"], a["v0"])
            experts(AT_PEER[1], a["u0"], a["v0"])
            stream(AT_HGIN, a["hgin"], N_HGIN)
            stream(AT_HGOUT, a["hgout"], N_OUT)
            stream(AT_WQ1, a["wq1"], N_WQ)
            experts(AT_PEER[2], a["u1"], a["v1"])
            sp.wait_ge(S["a_ready"], 5 * KD)
            sp.dma_start(out, A[:, :, 0:SEQ]).then_inc(S["out_done"], 16)
            sp.wait_ge(S["out_done"], 16)

        @block.gpsimd
        def _(pool):
            for dst, src in first:
                pool.dma_start(dst, src).then_inc(S["consts_in"], 16)
            pool.wait_ge(S["w_used"], AT_ABOUT + N_OUT)
            pool.dma_start(arena[:, 8192:10240], a["keys0"]).then_inc(S["keys_in"], 16)

            pool.wait_ge(S["ck_exp"], 1)
            pool.dma_start(arena[:, 30752:31776], a["masks"]).then_inc(S["masks_in"], 16)
            pool.wait_ge(S["w_used"], AT_HGOUT + N_OUT)
            pool.dma_start(arena[:, 8192:10240], a["keys1"]).then_inc(S["keys_in"], 16)

        @block.tensor
        def _(pe):
            def group(o, pairs, sem=None, **kw):
                for n, (l, r) in enumerate(pairs):
                    ins = pe.matmul(o, l, r, start=n == 0, stop=n == len(pairs) - 1, **kw)
                if sem is not None:
                    ins.then_inc(S[sem], 1)
                return ins

            def filters():
                pe.wait_ge(S["f_in"], 16 * len(filters_in))
                pe.wait_ge(S["consts_in"], 16 * len(first))
                group(ps[0:64, 0, 0:256], [(FW1, ZPOS)], "f_proj")
                pe.wait_ge(S["f_sin"], 1)
                group(ps[0:64, 1, 0:256], [(FW2, FHID[0])], "f_proj")
                pe.wait_ge(S["f_sin"], 2)
                for n in range(8):
                    wait(pe, S["f_rawtaken"], n - 1)
                    t, od = n // 4, n % 4
                    group(ps[:, 2 + n % 2, :], [(FHID[1][:, t * P:(t + 1) * P], FW3[:, od * 512:(od + 1) * 512])],
                          "f_raw")
                pe.wait_ge(S["f_abs"], 2)
                for o in range(2):
                    group(ps[:, 4 + o, :], [(ones[:, :], HABS[:, t, o, d, :]) for t in range(2) for d in range(2)],
                          "f_norm")
                pe.wait_ge(S["f_parts"], 1)
                for n in range(8):
                    o, q, f = n // 4, n // 2 % 2, n % 2
                    wait(pe, S["f_spectaken"], n - 1)
                    src, mat = (HSUM, COSF) if q == 0 else (HDIF, SINF)
                    group(ps[:, 6 + n % 2, :], [(mat[:, t, f * P:(f + 1) * P], src[:, o, t, :]) for t in range(2)],
                          "f_spec")

            def ada(g):
                m, count, pos = ADA_GROUPS[g]
                if g == 0:
                    pe.wait_ge(S["c_ready"], 1)
                    pe.wait_ge(S["f_spectaken"], 8)
                wait(pe, S["ada_taken"], g - 1 if g < 20 else g)
                for j in range(count):
                    n = pos + j
                    landed(pe, n)
                    group(ps[:, 5 + g % 2 if g < 20 else 5, 2 * j:2 * j + 2], [(W[:, n % RING, k, :], CS[:, k, :]) for k in range(KD)],
                          "w_used")

            def norm(k, width):
                for c in range(KD):
                    pe.wait_ge(S["sq_ready"], KD * k + c + 1)
                    ins = pe.matmul(ps[:, 7, 0:width], ones[:, :], SQ[:, c, 0:width], start=c == 0, stop=c == KD - 1)
                ins.then_inc(S["norm_summed"], 1)

            def ab_in():
                pe.wait_ge(S["a_ready"], KD)
                for j in range(N_ABIN):
                    n = at_abin(j)
                    wait(pe, S["ab_taken"], j - 3)
                    landed(pe, n)
                    o = ps[:, j % 4, :]
                    if j < 17:
                        group(o, [(W[:, n % RING, k, :], A[:, k, :]) for k in range(KD)], "w_used")
                    else:
                        for t in range(TT):
                            ins = group(o[:, t * P:(t + 1) * P],
                                        [(A[:, k, t * P:(t + 1) * P], W[:, n % RING, k, :]) for k in range(KD)])
                        ins.then_inc(S["w_used"], 1)
                    if j < 16:
                        ada(4 + j)

            def hyena():
                pe.wait_ge(S["ab_taken"], N_ABIN)
                for o in range(2):
                    z = UC if o == 0 else Z1
                    pe.wait_ge(S["cv_done"] if o == 0 else S["z_ready"], 1 if o == 0 else HC)
                    for t in range(TT):
                        for c in range(HC):
                            ins = pe.transpose(ps[:, t, c * P:(c + 1) * P], z[:, c, t * P:(t + 1) * P], ident[:, :])
                        ins.then_inc(S["zt_ready"], 1)
                    for n in range(4):
                        s, f = n // 2, n % 2
                        pe.wait_ge(S["zt_taken"], TT * o + 2 * (s + 1))
                        if n >= 2:
                            pe.wait_ge(S["pf_ready"], 4 * o + n - 1)
                        for q, mat in enumerate((COSF, SINF)):
                            ins = group(ps[:, 4 + 2 * (n % 2) + q, :],
                                        [(mat[:, t, f * P:(f + 1) * P], ZT[:, 2 * s + t, :]) for t in range(2)])
                        ins.then_inc(S["zf_ready"], 1)
                    pe.wait_ge(S["pf_ready"], 4 * (o + 1))
                    for c in range(HC):
                        for s in range(2):
                            ins = group(ps[:, c, s * SEQ:(s + 1) * SEQ],
                                        [(PF[:, s, q, f, c * P:(c + 1) * P], (COSG, SING)[q][:, f, :])
                                         for f in range(2) for q in range(2)])
                        ins.then_inc(S["yt_ready"], 1)

            def rope():
                pe.wait_ge(S["arena_in"], 16 * len(arena_loads))
                for j in range(5):
                    wait(pe, S["rope_done"], j - 1)
                    pe.matmul(ps[:, 4 + j % 2, 0:SEQ], ROT, QT[:, j, 0:SEQ] if j < 4 else KT[:, 0:SEQ],
                              start=True, stop=True).then_inc(S["rot_ready"], 1)

            def attention():
                pe.wait_ge(S["rope_done"], 5)
                pe.wait_ge(S["z_ready"], 2 * HC)

                def scores(u):
                    c, g, i = u // 8, u // 4 % 2, u % 4
                    wait(pe, S["sc_taken"], u - 1)
                    keys = KT[64 * g:64 * g + 64, :] if i < 2 else KT[64 * g:64 * g + 64, SEQ:T]
                    pe.matmul(ps[:, u % 2, 0:512 if i < 2 else 256], QT[64 * g:64 * g + 64, c, i * P:(i + 1) * P],
                              keys, start=True, stop=True).then_inc(S["sc_ready"], 1)

                def turn(u):
                    i = u % 4
                    pe.wait_ge(S["pn_ready"], u + 1)
                    wait(pe, S["pt_taken"], u - 1)
                    for k in range(4 if i < 2 else 2):
                        ins = pe.transpose(ps[:, 2 + u % 2, k * P:(k + 1) * P], APR[:, u % 2, k * P:(k + 1) * P],
                                           ident[:, :])
                    ins.then_inc(S["pt_ready"], 1)

                def values(u):
                    c, g, i = u // 8, u // 4 % 2, u % 4
                    pe.wait_ge(S["pt_taken"], u + 1)
                    if u % 8 == 0:
                        wait(pe, S["att_done"], c - 1)
                    k0, kn = (0, 4) if i < 2 else (2, 2)
                    group(ps[64 * g:64 * g + 64, 4 + c % 2, i * P:(i + 1) * P],
                          [(VT[:, k0 + k, 64 * g:64 * g + 64], APT[:, u % 2, k, :]) for k in range(kn)], "pv_done")

                scores(0)
                for u in range(34):
                    if u + 1 < 32:
                        scores(u + 1)
                    if 1 <= u < 33:
                        turn(u - 1)
                    if u >= 2:
                        values(u - 2)

            def mixer_out(l, n0, src, width):
                for c in range(KD):
                    n = n0 + c
                    wait(pe, S["h_ready"], (0, 3 * KD)[l] + c - 3 if c >= 4 else 0)
                    landed(pe, n)
                    group(ps[:, c % 4, 0:width], [(W[:, n % RING, k, :], src[:, k, :]) for k in range(KD)], "w_used")

            def queries(l, width):
                pe.wait_ge(S["a_ready"], (2, 4)[l] * KD)
                for j in range(N_WQ):
                    n = at_wq(l, j)
                    wait(pe, S["wq_taken"], N_WQ * l + j - 3 if j >= 4 else 0)
                    landed(pe, n)
                    group(ps[:, j % 4, 0:width], [(W[:, n % RING, k, :], A[:, k, 0:width]) for k in range(KD)],
                          "w_used")

            def routing(l, tiles):
                pe.wait_ge(S["keys_in"], 16 * (l + 1))
                base = (0, TT)[l]

                def scores(i):
                    pe.wait_ge(S["qc_ready"], base + i + 1)
                    for j in range(16):
                        ins = pe.matmul(ps[:, j // 4, j % 4 * P:(j % 4 + 1) * P], PQC[:, j, :], KEYS[:, j, :],
                                        start=True, stop=True)
                    ins.then_inc(S["route_scores"], 1)

                scores(0)
                for i in range(tiles):
                    if l == 0:
                        ada(20 + i)
                    if i + 1 < tiles:
                        scores(i + 1)
                    pe.wait_ge(S["gates_ready"], base + i + 1)
                    for q in range(3):
                        ins = pe.transpose(ps[:, 4, q * P:(q + 1) * P],
                                           GATE[:, q, :, :].rearrange("p h k -> p (h k)"), ident[:, :])
                    ins.then_inc(S["slots_t"], 1)

            def gates(n, i=0):
                pe.wait_ge(S["oh_ready"], i * 4 + (n + 1))
                wait(pe, S["g_taken"], i * 4 + (n - 1))
                for u in range(GTOK):
                    ins = pe.matmul(ps[:, 2 + n % 2, 2 * u * QKEYS:2 * (u + 1) * QKEYS], OHB[:, n % 2, u, :],
                                    OHA[:, n % 2, u, :, :].rearrange("p q e -> p (q e)"), start=True, stop=True)
                ins.then_inc(S["oh_used"], 1)

            def first_quarter(n0):
                for g in range(4):
                    gates(n0 + g)
                with pe.Fori(1, GROUPS // 4) as i:
                    for g in range(4):
                        gates(n0 + g, i)

            def parts(hi, lo, x_hi, x_lo):
                return [(hi, x_hi), (hi, x_lo), (lo, x_hi)]

            def experts(p):
                n0, k0, m0, g0 = AT_PEER[p], p * N_PEER, p * NKEY, PASS_GROUP[p]

                def first_half(m, slot, i=0):
                    k = tile_u(m)
                    pe.wait_ge(S["w_used"], i * TURN + (n0 + k + 1))
                    wait(pe, S["gelu_done"], i * 4 + (m0 + m - 1))
                    r = k % 4
                    group(ps[:, slot % 2, 0:SEQ],
                          [x for c in range(KD) for x in parts(WHI[:, r, c, :], WLO[:, r, c, :], XHI[:, c, :], XLO[:, c, :])],
                          "part_used")

                def second_half(m, i=0):
                    k = tile_v(m)
                    pe.wait_ge(S["w_used"], i * TURN + (n0 + k + 1))
                    pe.wait_ge(S["act_ready"], i * 4 + (m0 + m + 1))
                    begin, end = (isinstance(i, int) and m == x for x in (0, NKEY - 1))
                    r, b = k % 4, m % 2
                    for c in range(KD):
                        out_c = ps[:, 4 + c // 2, c % 2 * SEQ:(c % 2 + 1) * SEQ]
                        for n, (w, x) in enumerate(parts(WHI[:, r, c, :], WLO[:, r, c, :], ACH[:, b, :], ACL[:, b, :])):
                            ins = pe.matmul(out_c, w, x, start=begin and c % 2 == 0 and n == 0, stop=end and n == 2,
                                            skip_group_check=True)
                    ins.then_inc(S["part_used"], 1)

                def turn(q, i, e0):
                    for e in range(e0, e0 + 4):
                        if e + 1 < NKEY:
                            first_half(e + 1, e + 1, i)
                        if p == 0 or q < QUARTERS - 1:
                            gates(g0 + e, i)
                        if p == 1 and isinstance(i, int) and e == 0:
                            pe.wait_ge(S["h_ready"], 2 * KD)
                        second_half(e, i)

                pe.wait_ge(S["x_ready"], KD * (p + 1))
                first_half(0, 0)
                turn(0, 0, 0)
                if p == 0:
                    with pe.Fori(1, NKEY // 4 - 1) as i:
                        turn(0, i, 0)
                else:
                    with pe.Fori(1, 3 * QKEYS // 4) as i:
                        turn(0, i, 0)
                    with pe.Fori(0, QKEYS // 4 - 1) as i:
                        turn(3, i, 3 * QKEYS)
                turn(3, 0, NKEY - 4)

            def hg_in():
                pe.wait_ge(S["a_ready"], 3 * KD)
                for j in range(N_HGIN):
                    n = AT_HGIN + j
                    wait(pe, S["hg_taken"], j - 3)
                    landed(pe, n)
                    o = ps[:, j % 4, :]
                    if 24 <= j < 32:
                        for t in range(TT):
                            ins = group(o[:, t * P:(t + 1) * P],
                                        [(A[:, k, t * P:(t + 1) * P], W[:, n % RING, k, :]) for k in range(KD)])
                        ins.then_inc(S["w_used"], 1)
                    else:
                        width = T if 8 <= j < 24 else SEQ
                        group(o[:, 0:width], [(W[:, n % RING, k, :], A[:, k, 0:width]) for k in range(KD)], "w_used")

            def states():
                pe.wait_ge(S["hg_taken"], N_HGIN)
                pe.wait_ge(S["ck_ready"], 3)
                for n in range(8):
                    t, d, hh = n // 4, n // 2 % 2, n % 2
                    wait(pe, S["ck_in"], n - 3)
                    for h in range(4):
                        ins = pe.transpose(ps[:, n % 4, h * P:(h + 1) * P], CK[:, d, 4 * hh + h, t * P:(t + 1) * P],
                                           ident[:, :])
                    ins.then_inc(S["ck_t"], 1)
                pe.wait_ge(S["ck_in"], 8)
                for n in range(4):
                    d, hh = n // 2, n % 2
                    for h in range(4):
                        hd = 4 * hh + h
                        ins = group(ps[:, 4 + n, h * P:(h + 1) * P],
                                    [(CKT[:, t, d, hd, :], IV[:, 2 + t, hd, :]) for t in range(2)])
                    ins.then_inc(S["cs_ready"], 1)
                pe.wait_ge(S["lk_ready"], 2)
                for n in range(4):
                    d, hh = n // 2, n % 2
                    for h in range(4):
                        ins = pe.transpose(ps[:, n, h * P:(h + 1) * P], LK[:, d, 4 * hh + h, :], ident[:, :])
                    ins.then_inc(S["lk_t"], 1)
                pe.wait_ge(S["cs_taken"], 4)
                pe.wait_ge(S["lk_in"], 4)
                for n in range(4):
                    d, hh = n // 2, n % 2
                    for h in range(4):
                        hd = 4 * hh + h
                        ins = group(ps[:, 4 + n, h * P:(h + 1) * P], [(LKT[:, d, hd, :], IV[:, d, hd, :])])
                    ins.then_inc(S["ls_ready"], 1)

            def levels():
                for lv in range(LEVELS + 1):
                    pe.wait_ge(S["lv_ready"], lv + 1)
                    wait(pe, S["lv_taken"], 4 * lv)
                    q, k = LV[lv % 2]
                    for b in range(4):
                        for m in range(4):
                            ins = pe.matmul(ps[:, b, m * P:(m + 1) * P], k[:, 4 * b + m, :], q[:, 4 * b + m, :],
                                            start=True, stop=True)
                        ins.then_inc(S["lv_prod"], 1)
                pe.wait_ge(S["lv_taken"], 4 * (LEVELS + 1))
                pe.wait_ge(S["ls_done"], 4)
                pe.wait_ge(S["qi_ready"], 2)
                for h in range(NH):
                    for t in range(2):
                        cols = slice(h % 2 * SEQ + t * P, h % 2 * SEQ + (t + 1) * P)
                        ins = group(ps[:, 4 + h // 2, cols],
                                    [(ST[:, t, 0, h, :], QI[:, 0, h, t * P:(t + 1) * P]),
                                     (ST[:, 1 - t, 1, h, :], QI[:, 1, h, t * P:(t + 1) * P]),
                                     (IV[:, t, h, :], AT_[:, 2 * h + t, :])])
                    if h % 2:
                        ins.then_inc(S["oi_ready"], 1)
                for b in range(4):
                    pe.wait_ge(S["osq_ready"], b + 1)
                    pe.matmul(ps[:, b, :], ones[:, :], OSQ[:, 2 * b:2 * b + 2, :].rearrange("p h t -> p (h t)"),
                              start=True, stop=True).then_inc(S["ors_ready"], 1)

            filters()
            for g in range(4):
                ada(g)
            norm(0, T)
            ab_in()
            hyena()
            rope()
            attention()
            pe.wait_ge(S["att_done"], 4)
            mixer_out(0, AT_ABOUT, MIX, T)
            norm(1, T)
            queries(0, T)
            routing(0, TT)
            first_quarter(0)
            experts(0)
            experts(1)
            norm(2, T)
            hg_in()
            states()
            levels()
            pe.wait_ge(S["mx_ready"], 4)
            mixer_out(1, AT_HGOUT, MX1, SEQ)
            norm(3, SEQ)
            queries(1, SEQ)
            routing(1, CHUNKS)
            first_quarter(2 * QUARTERS * GROUPS)
            experts(2)
            norm(4, SEQ)

        @block.scalar
        def _(act):
            for dst, src in filters_in:
                act.dma_start(dst, src).then_inc(S["f_in"], 16)
            for dst, src in arena_loads:
                act.dma_start(dst, src).then_inc(S["arena_in"], 16)
            copy = nc.scalar.copy

            act.wait_ge(S["consts_in"], 16 * len(first))
            act.activation(csil[:, :], csil[:, :], ACT.Silu).then_inc(S["c_ready"], 1)

            def filters():
                for n in range(2):
                    act.wait_ge(S["f_arg"], n + 1)
                    act.activation(FHID[n], FARG, ACT.Sin).then_inc(S["f_sin"], 1)
                for t in range(2):
                    act.wait_ge(S["f_rawtaken"], 4 * (t + 1))
                    act.activation(HABS[:, t].rearrange("p o d c -> p (o d c)"),
                                   HRAW[:, t].rearrange("p o d c -> p (o d c)"), ACT.Abs).then_inc(S["f_abs"], 1)

            def norm(k, width, streams):
                for c in range(KD):
                    act.activation(SQ[:, c, 0:width], H[:, c, 0:width], ACT.Square).then_inc(S["sq_ready"], 1)
                act.wait_ge(S["ms_ready"], k + 1)
                act.activation(rstd[:, 0:width], rstd[:, 0:width], ACT.Sqrt).then_inc(S["std_ready"], 1)
                if k < 4:
                    act.wait_ge(S["mods_ready"], k + 1)
                for c in range(KD):
                    act.wait_ge(S["hn_ready"], KD * k + c + 1)
                    for s in range(streams):
                        cols = slice(s * SEQ, (s + 1) * SEQ)
                        if k < 4:
                            ins = act.activation(A[:, c, cols], SQ[:, c, cols], ACT.Identity,
                                                 scale=GM[:, k, c, s:s + 1], bias=M[:, k // 2, k % 2 * 3, c, s:s + 1])
                        else:
                            ins = act.activation(A[:, c, cols], SQ[:, c, cols], ACT.Identity, scale=GN[:, 4, c:c + 1])
                    ins.then_inc(S["a_ready"], 1)

            def ab_in():
                for j in range(N_ABIN):
                    act.wait_ge(S["w_used"], at_abin(j) + 1)
                    dst = U[:, j, :] if j < 12 else QT[:, j - 12, :] if j < 16 else KT if j == 16 else \
                        VT.rearrange("p t n -> p (t n)")
                    copy(dst, ps[:, j % 4, :]).then_inc(S["ab_taken"], 1)
                for j in range(12):
                    if j == 0:
                        act.wait_ge(S["ab_taken"], 12)
                    act.activation(UC[:, j, :], U[:, j, :], ACT.Identity, scale=conv[:, 12 + j:13 + j],
                                   bias=conv[:, 36 + j:37 + j]).then_inc(S["cv_mid"], 1)

            def hyena():
                for o in range(2):
                    for t in range(TT):
                        act.wait_ge(S["zt_ready"], TT * o + t + 1)
                        copy(ZT[:, t, :], ps[:, t, :]).then_inc(S["zt_taken"], 1)

            def attention():
                def exps(u):
                    c, g, i = u // 8, u // 4 % 2, u % 4
                    h = 4 * g + c
                    n = 512 if i < 2 else 256
                    act.wait_ge(S["nmax_ready"], u + 1)
                    wait(act, S["pt_ready"], u - 1)
                    r = 4 * (u % 2)
                    act.activation(APR[:, u % 2, 0:n], ASC[:, u % 2, 0:n], ACT.Exp, bias=small[:, r:r + 1],
                                   scale=HD ** -0.5, accum_out=small[:, r + 1:r + 2])
                    act.activation(small[:, r + 2:r + 3], sinks[:, h:h + 1], ACT.Exp, bias=small[:, r:r + 1])\
                        .then_inc(S["exp_ready"], 1)

                def turned(u):
                    i = u % 4
                    n = 512 if i < 2 else 256
                    act.wait_ge(S["pt_ready"], u + 1)
                    wait(act, S["pv_done"], u - 1)
                    copy(APT[:, u % 2].rearrange("p k q -> p (k q)")[:, 0:n], ps[:, 2 + u % 2, 0:n])\
                        .then_inc(S["pt_taken"], 1)

                for u in range(35):
                    if u < 32:
                        exps(u)
                    if 1 <= u < 33:
                        turned(u - 1)
                    if u >= 3 and (u - 3) % 8 == 7:
                        c = (u - 3) // 8
                        act.wait_ge(S["pv_done"], 8 * (c + 1))
                        copy(MIX[:, 4 + c, :], ps[:, 4 + c % 2, :]).then_inc(S["att_done"], 1)

            def queries(l, width):
                for j in range(N_WQ):
                    act.wait_ge(S["w_used"], at_wq(l, j) + 1)
                    copy(PQT[:, j, 0:width], ps[:, j % 4, 0:width]).then_inc(S["wq_taken"], 1)

            def routing(l, tiles):
                base = (0, TT)[l]
                act.wait_ge(S["wq_taken"], N_WQ * (l + 1))

                def queries_in(i):
                    copy(PQC, PQT[:, :, bass.ds(i * P, P)]).then_inc(S["qc_ready"], 1)
                    act.wait_ge(S["route_scores"], i + (base + 1))
                    wait(act, S["scores_used"], i + base)
                    copy(PS1.rearrange("p (b j) n -> p b (j n)", b=4), ps[:, 0:4, :]).then_inc(S["scores_ready"], 1)

                def exps(i):
                    act.wait_ge(S["diff_ready"], i + (base + 1))
                    act.activation(GATE[:, 0, :, :], GATE[:, 0, :, :], ACT.Exp).then_inc(S["gate_exp"], 1)

                def turned(i):
                    act.wait_ge(S["slots_t"], i + (base + 1))
                    copy(SL[:, :, bass.ds(i * P, P)], ps[:, 4, 0:3 * P].rearrange("p (q t) -> p q t", q=3))\
                        .then_inc(S["slots_in"], 1)

                queries_in(0)
                with act.Fori(0, tiles - 1) as i:
                    exps(i)
                    queries_in(i + 1)
                    turned(i)
                exps(tiles - 1)
                turned(tiles - 1)

            def gates_high(n, buf, g, i=0):
                act.wait_ge(S["oh_used"], i * 4 + (n + 1))
                copy(G[:, buf, :, bass.ds(i * 4 * GTOK + g * GTOK, GTOK)], gate_sums(n)[:, 0]).then_inc(S["g_high"], 1)

            def first_quarter(n0):
                for g in range(4):
                    gates_high(n0 + g, 0, g)
                with act.Fori(1, GROUPS // 4) as i:
                    for g in range(4):
                        gates_high(n0 + g, 0, g, i)

            def high(p, k, i=0):
                n = AT_PEER[p] + k
                landed(act, n, i)
                wait(act, S["part_used"], i * TURN + (p * N_PEER + k - 3))
                copy(WHI[:, k % 4].rearrange("p k n -> p (k n)"), wring[:, n % RING * TILE:(n % RING + 1) * TILE])\
                    .then_inc(S["hi_ready"], 1)

            def operands(p):
                wait(act, S["part_used"], p * N_PEER)
                t0 = PASS_TOK[p]
                for c in range(KD):
                    copy(XHI[:, c, :], A[:, c, t0:t0 + SEQ]).then_inc(S["xhi_ready"], 1)
                for k in range(3):
                    high(p, k)

            def experts(p):
                k0, m0, g0 = p * N_PEER, p * NKEY, PASS_GROUP[p]

                def turn(q, i, e0):
                    for m in range(e0, e0 + 4):
                        act.wait_ge(S["part_used"], i * TURN + (k0 + tile_u(m) + 1) if isinstance(i, int) or m else
                                    i * TURN + k0)
                        wait(act, S["act_ready"], i * 4 + (m0 + m - 1))
                        act.activation(GL[:, m % 2, :], ps[:, m % 2, 0:SEQ], ACT.Gelu).then_inc(S["gelu_done"], 1)
                        if m + 2 < NKEY:
                            high(p, tile_u(m + 2), i)
                        act.wait_ge(S["mul_ready"], i * 4 + (m0 + m + 1))
                        copy(ACH[:, m % 2, :], GL[:, m % 2, :]).then_inc(S["acthi_ready"], 1)
                        if m + 1 < NKEY:
                            high(p, tile_v(m + 1), i)
                        if p == 0 or q < QUARTERS - 1:
                            gates_high(g0 + m, (q + 1) % 2, m % QKEYS, i)

                quarters(act, turn)

            def hg_in():
                for j in range(N_HGIN):
                    act.wait_ge(S["w_used"], AT_HGIN + j + 1)
                    src = ps[:, j % 4, :]
                    if j < 8:
                        ins = act.activation(RQ[:, j, :], src[:, 0:SEQ], ACT.Silu)
                    elif j < 24:
                        ins = act.activation(LF[:, j - 8, :], src, ACT.Sigmoid)
                    elif j < 32:
                        ins = copy(IV[:, :, j - 24, :], src.rearrange("p (t n) -> p t n", t=TT))
                    else:
                        ins = act.activation(RG[:, j - 32, :], src[:, 0:SEQ], ACT.Silu)
                    ins.then_inc(S["hg_taken"], 1)
                act.wait_ge(S["fk_done"], 16)
                act.activation(LF.rearrange("p m t -> p (m t)"), LF.rearrange("p m t -> p (m t)"), ACT.Ln)\
                    .then_inc(S["ln_done"], 1)

            def states():
                act.wait_ge(S["scan_done"], 1)
                for h in range(NH):
                    act.activation(CK[:, 0, h, :], EC[:, 0, h, :], ACT.Exp, scale=-1.0, bias=EC[:, 0, h, SEQ - 1:SEQ])
                act.activation(CK[:, 1], EC[:, 1], ACT.Exp).then_inc(S["ck_exp"], 1)
                for n in range(8):
                    t, d, hh = n // 4, n // 2 % 2, n % 2
                    act.wait_ge(S["ck_t"], n + 1)
                    copy(CKT[:, t, d, 4 * hh:4 * hh + 4, :].rearrange("p h n -> p (h n)"), ps[:, n % 4, :])\
                        .then_inc(S["ck_in"], 1)
                act.wait_ge(S["ck_t"], 8)
                for h in range(NH):
                    act.activation(LK[:, 0, h, :], EL[:, 0, 2 * h, 1:129], ACT.Exp, scale=-1.0,
                                   bias=EL[:, 0, 2 * h, 128:129])
                    ins = act.activation(LK[:, 1, h, :], EL[:, 1, 2 * h + 1, 0:128], ACT.Exp)
                ins.then_inc(S["lk_exp"], 1)
                for h in range(NH):
                    for t in range(2):
                        m = 2 * h + t
                        act.activation(QI[:, 0, h, t * P:(t + 1) * P], EL[:, 0, m, 1:129], ACT.Exp)
                        ins = act.activation(QI[:, 1, h, t * P:(t + 1) * P], EL[:, 1, m, 0:128], ACT.Exp, scale=-1.0,
                                             bias=EL[:, 1, m, 128:129])
                ins.then_inc(S["qi_exp"], 1)
                for n in range(4):
                    d, hh = n // 2, n % 2
                    act.wait_ge(S["cs_ready"], n + 1)
                    copy(ST[:, 0, d, 4 * hh:4 * hh + 4, :].rearrange("p h n -> p (h n)"), ps[:, 4 + n, :])\
                        .then_inc(S["cs_taken"], 1)
                act.wait_ge(S["dec_in"], 1)
                act.activation(lbs[:, 16:32], lbs[:, 0:16], ACT.Exp).then_inc(S["dec_exp"], 1)
                act.wait_ge(S["cs_ready"], 4)
                for n in range(4):
                    d, hh = n // 2, n % 2
                    act.wait_ge(S["lk_t"], n + 1)
                    copy(LKT[:, d, 4 * hh:4 * hh + 4, :].rearrange("p h n -> p (h n)"), ps[:, n, :])\
                        .then_inc(S["lk_in"], 1)

            def levels():
                for lv in range(LEVELS):
                    act.wait_ge(S["lv_diff"], lv + 1)
                    for b in LV[lv % 2]:
                        ins = act.activation(b, b, ACT.Exp)
                    ins.then_inc(S["lv_exp"], 1)
                for b in range(4):
                    act.wait_ge(S["oi_ready"], b + 1)
                    act.activation(OSQ[:, 2 * b:2 * b + 2, :].rearrange("p h t -> p (h t)"), ps[:, 4 + b, :], ACT.Square)\
                        .then_inc(S["osq_ready"], 1)
                act.wait_ge(S["oms_ready"], 4)
                act.activation(ORS, ORS, ACT.Sqrt).then_inc(S["ostd_ready"], 1)

            act.wait_ge(S["lb_diff"], 2)
            act.activation(lbs[:, 32:64], lbs[:, 32:64], ACT.Exp).then_inc(S["lb_exp"], 1)
            filters()
            act.wait_ge(S["x_in"], 16)
            norm(0, T, 2)
            ab_in()
            hyena()
            attention()
            act.wait_ge(S["h_ready"], KD)
            norm(1, T, 2)
            queries(0, T)
            routing(0, TT)
            operands(0)
            first_quarter(0)
            experts(0)
            operands(1)
            experts(1)
            act.wait_ge(S["h_ready"], 3 * KD)
            norm(2, T, 2)
            hg_in()
            states()
            levels()
            act.wait_ge(S["h_ready"], 4 * KD)
            norm(3, SEQ, 1)
            queries(1, SEQ)
            routing(1, CHUNKS)
            operands(2)
            first_quarter(2 * QUARTERS * GROUPS)
            experts(2)
            act.wait_ge(S["h_ready"], 5 * KD)
            norm(4, SEQ, 1)

        @block.vector
        def _(dve):
            step = Chain(dve, S["dve_step"], settle_dve)
            tt, ts, stt = dve.tensor_tensor, dve.tensor_scalar, dve.scalar_tensor_tensor

            def bounds():
                l0, l1 = lbs[:, 0:16], lbs[:, 16:32]
                step.done(tt(lbs[:, 64:80], l0, l1, ALU.max))
                for n in range(2):
                    tt(lbs[:, 32 + 16 * n:48 + 16 * n], lbs[:, 16 * n:16 * n + 16], lbs[:, 64:80], ALU.subtract)\
                        .then_inc(S["lb_diff"], 1)
                dve.wait_ge(S["lb_exp"], 1)
                step.done(tt(lbs[:, 80:96], lbs[:, 32:48], lbs[:, 48:64], ALU.add))
                step.done(dve.reciprocal(lbs[:, 80:96], lbs[:, 80:96]))
                for n in range(2):
                    step.done(tt(lbs[:, 32 + 16 * n:48 + 16 * n], lbs[:, 32 + 16 * n:48 + 16 * n], lbs[:, 80:96],
                                 ALU.mult))
                step.done(tt(lbs[:, 96:112], lbs[:, 32:48], lbs[:, 48:64], ALU.add))
                step.done(tt(lbs[:, 96:112], lbs[:, 96:112], lbs[:, 32:48], ALU.subtract))
                step.done(ts(lbs[:, 112:128], lbs[:, 96:112], -1.0, 1.0, ALU.mult, ALU.add))

            def filters():
                dve.wait_ge(S["f_in"], 16 * len(filters_in))
                for n in range(2):
                    dve.wait_ge(S["f_proj"], n + 1)
                    step.done(ts(FARG, ps[0:64, n, 0:256], filt[0:64, n:n + 1], filt[0:64, 2:3], ALU.add, ALU.mult))
                    step.done(ts(FRND, FARG, 1.0 / TWO_PI, ROUND, ALU.mult, ALU.add))
                    step.done(ts(FRND, FRND, ROUND, None, ALU.subtract))
                    for part in (PI_A, PI_B, PI_C):
                        step.done(stt(FARG, FRND, -part, FARG, ALU.mult, ALU.add))
                    ts(FARG, FARG, 3.1415925, -3.1415925, ALU.min, ALU.max).then_inc(S["f_arg"], 1)
                for n in range(8):
                    t, od = n // 4, n % 4
                    dve.wait_ge(S["f_raw"], n + 1)
                    tt(HRAW[:, t, od // 2, od % 2, :], ps[:, 2 + n % 2, :], DECAY[:, t, :], ALU.mult)\
                        .then_inc(S["f_rawtaken"], 1)
                dve.wait_ge(S["f_abs"], 2)
                dve.wait_ge(S["f_rawtaken"], 8)
                for o in range(2):
                    step.done(dve.memset(HRAW[0:1, 0, o, 1, :], 0.0))
                for o in range(2):
                    for t in range(2):
                        tt(HSUM[:, o, t, :], HRAW[:, t, o, 0, :], HRAW[:, t, o, 1, :], ALU.add)
                        ins = tt(HDIF[:, o, t, :], HRAW[:, t, o, 0, :], HRAW[:, t, o, 1, :], ALU.subtract)
                ins.then_inc(S["f_parts"], 1)
                for o in range(2):
                    dve.wait_ge(S["f_norm"], o + 1)
                    step.done(dve.reciprocal(RNRM[:, o, :], ps[:, 4 + o, :]))
                for n in range(8):
                    o, q, f = n // 4, n // 2 % 2, n % 2
                    dve.wait_ge(S["f_spec"], n + 1)
                    tt(HF[:, o, q, f, :], ps[:, 6 + n % 2, :], RNRM[:, o, :], ALU.mult).then_inc(S["f_spectaken"], 1)

            def ada(g):
                m, count, pos = ADA_GROUPS[g]
                dve.wait_ge(S["w_used"], pos + count)
                tt(M2[:, m:m + count, :], ps[:, 5 + g % 2, 0:2 * count].rearrange("p (m z) -> p m z", z=2),
                   adab[:, m:m + count].unsqueeze(2).to_broadcast([P, count, 2]), ALU.add).then_inc(S["ada_taken"], 1)

            def gains_of(norms, groups):
                dve.wait_ge(S["ada_taken"], groups)
                for n in norms:
                    stt(GM[:, n], M[:, n // 2, n % 2 * 3 + 1], 1.0, GN[:, n, :].unsqueeze(2).to_broadcast([P, KD, 2]),
                        ALU.add, ALU.mult).then_inc(S["mods_ready"], 1)

            def norm(k, width):
                dve.wait_ge(S["norm_summed"], k + 1)
                ts(rstd[:, 0:width], ps[:, 7, 0:width], 1.0 / D, EPS, ALU.mult, ALU.add).then_inc(S["ms_ready"], 1)
                dve.wait_ge(S["std_ready"], k + 1)
                step.done(dve.reciprocal(rstd[:, 0:width], rstd[:, 0:width]))
                for c in range(KD):
                    tt(SQ[:, c, 0:width], H[:, c, 0:width], rstd[:, 0:width], ALU.mult).then_inc(S["hn_ready"], 1)

            def short_conv():
                ucs = UC.rearrange("p j (s t) -> p j s t", s=2)
                us = U.rearrange("p j (s t) -> p j s t", s=2)
                for j in range(12):
                    dve.wait_ge(S["cv_mid"], j + 1)
                    stt(ucs[:, j, :, 1:SEQ], us[:, j, :, 0:SEQ - 1], conv[:, j:j + 1], ucs[:, j, :, 1:SEQ],
                        ALU.mult, ALU.add).then_inc(S["dve_step"], 1)
                step.n += 12
                dve.wait_ge(S["dve_step"], step.n)
                for j in range(12):
                    ins = stt(ucs[:, j, :, 0:SEQ - 1], us[:, j, :, 1:SEQ], conv[:, 24 + j:25 + j],
                              ucs[:, j, :, 0:SEQ - 1], ALU.mult, ALU.add)
                ins.then_inc(S["cv_done"], 1)
                dve.wait_ge(S["cv_done"], 1)

            def hyena():
                for o in range(2):
                    z = UC if o == 0 else Z1
                    for n in range(4):
                        s, f = n // 2, n % 2
                        dve.wait_ge(S["zf_ready"], 4 * o + n + 1)
                        if o == 1 and n == 0:
                            dve.wait_ge(S["yt_ready"], HC)
                        zc, zs = ps[:, 4 + 2 * (n % 2), :], ps[:, 5 + 2 * (n % 2), :]
                        hc, hs = HF[:, o, 0, f, :], HF[:, o, 1, f, :]
                        t0, t1 = RTMP[:, 0:512], hand[:, 512:1024]
                        tt(PF[:, s, 0, f, :], zc, hc, ALU.mult)
                        tt(PF[:, s, 1, f, :], zc, hs, ALU.mult)
                        tt(t0, zs, hs, ALU.mult)
                        step.done(tt(t1, zs, hc, ALU.mult))
                        tt(PF[:, s, 0, f, :], PF[:, s, 0, f, :], t0, ALU.subtract)
                        ins = tt(PF[:, s, 1, f, :], PF[:, s, 1, f, :], t1, ALU.add)
                        ins.then_inc(S["pf_ready"], 1)
                        dve.wait_ge(S["pf_ready"], 4 * o + n + 1)
                    for c in range(HC):
                        dve.wait_ge(S["yt_ready"], HC * o + c + 1)
                        dst = Z1[:, c, :] if o == 0 else MIX[:, c, :]
                        step.done(stt(RTMP, z[:, c, :], dskip[:, HC * o + c:HC * o + c + 1], ps[:, c, :],
                                      ALU.mult, ALU.add))
                        tt(dst, RTMP, UC[:, 4 * (o + 1) + c, :], ALU.mult).then_inc(S["z_ready"], 1)
                        dve.wait_ge(S["z_ready"], HC * o + c + 1)

            def rope():
                dve.wait_ge(S["arena_in"], 32)
                for j in range(5):
                    x = QT[:, j, 0:SEQ] if j < 4 else KT[:, 0:SEQ]
                    dve.wait_ge(S["rot_ready"], j + 1)
                    step.done(tt(RTMP[:, 0:SEQ], ps[:, 4 + j % 2, 0:SEQ], ROPE[:, 1, :], ALU.mult))
                    step.done(tt(x, x, ROPE[:, 0, :], ALU.mult))
                    tt(x, x, RTMP[:, 0:SEQ], ALU.add).then_inc(S["rope_done"], 1)
                    dve.wait_ge(S["rope_done"], j + 1)

            def attention():
                step.done(ts(sinks[:, NQ:2 * NQ], sinks[:, 0:NQ], -1.0, None, ALU.mult))

                def maxima(u):
                    c, g, i = u // 8, u // 4 % 2, u % 4
                    h = 4 * g + c
                    n = 512 if i < 2 else 256
                    r = 4 * (u % 2)
                    dve.wait_ge(S["sc_ready"], u + 1)
                    wait(dve, S["exp_ready"], u - 1)
                    if i < 2:
                        ins = tt(ASC[:, u % 2, 0:n], ps[:, u % 2, 0:n], AMASK[:, i, :], ALU.add)
                    else:
                        ins = dve.tensor_copy(ASC[:, u % 2, 0:n], ps[:, u % 2, 0:n])
                    ins.then_inc(S["sc_taken"], 1)
                    dve.wait_ge(S["sc_taken"], u + 1)
                    step.done(dve.tensor_reduce(small[:, r + 3:r + 4], ASC[:, u % 2, 0:n], AXX, ALU.max, negate=True))
                    ts(small[:, r:r + 1], small[:, r + 3:r + 4], HD ** -0.5, sinks[:, NQ + h:NQ + h + 1],
                       ALU.mult, ALU.min).then_inc(S["nmax_ready"], 1)

                def normalise(u):
                    i = u % 4
                    n = 512 if i < 2 else 256
                    r = 4 * (u % 2)
                    dve.wait_ge(S["exp_ready"], u + 1)
                    step.done(tt(small[:, r + 2:r + 3], small[:, r + 1:r + 2], small[:, r + 2:r + 3], ALU.add))
                    step.done(dve.reciprocal(small[:, r + 2:r + 3], small[:, r + 2:r + 3]))
                    ts(APR[:, u % 2, 0:n], APR[:, u % 2, 0:n], small[:, r + 2:r + 3], None, ALU.mult)\
                        .then_inc(S["pn_ready"], 1)

                for u in range(33):
                    if u < 32:
                        maxima(u)
                    if u >= 1:
                        normalise(u - 1)

            def residual(l, kind, n0, bank, width, streams, ready):
                for c in range(KD):
                    ready(c)
                    for s in streams:
                        cols = slice(s * SEQ, (s + 1) * SEQ)
                        ins = stt(H[:, c, cols], bank(c, s), M[:, l, kind, c, s:s + 1], H[:, c, cols], ALU.mult, ALU.add)
                    ins.then_inc(S["h_ready"], 1)

            def routing(l, tiles):
                base = (0, TT)[l]
                n0 = step.n

                def wide(t, shape):
                    return t.to_broadcast(shape)

                def top(count, vals, vals2, tops, idx):
                    for j in range(count):
                        ins = dve.max(tops[:, j, 0:8], vals[:, j, :])
                    step.done(ins)
                    for j in range(count):
                        dve.max_index(idx[:, j, 0:8], tops[:, j, 0:8], vals[:, j, :])
                        ins = dve.match_replace(vals2[:, j, :], tops[:, j, 0:8], vals[:, j, :], NEG)
                    step.done(ins)
                    for j in range(count):
                        ins = dve.max(tops[:, j, 8:16], vals2[:, j, :])
                    step.done(ins)
                    for j in range(count):
                        ins = dve.max_index(idx[:, j, 8:16], tops[:, j, 8:16], vals2[:, j, :])
                    step.done(ins)

                with dve.Fori(0, tiles) as i:
                    step.enter(i, ROUTE_STEPS)
                    dve.wait_ge(S["scores_ready"], i + (base + 1))
                    settle_dve()
                    top(16, PS1, PS2, TV, TIU)
                    dve.tensor_copy(TIF, TIU).then_inc(S["scores_used"], 1)
                    tv = TV.rearrange("p (h q) k -> p h q k", q=2)
                    step.done(tt(CAND.rearrange("p h (i j) -> p h i j", i=TOPK),
                                 wide(tv[:, :, 0, :].unsqueeze(3), [P, NH, TOPK, TOPK]),
                                 wide(tv[:, :, 1, :].unsqueeze(2), [P, NH, TOPK, TOPK]), ALU.add))
                    top(NH, CAND, CAN2, SV, SJU)
                    tt(GATE[:, 0], SV, wide(SV[:, :, 0:1], [P, NH, TOPK]), ALU.subtract).then_inc(S["diff_ready"], 1)
                    ts(HIU[:, 0], SJU, 4, None, ALU.logical_shift_right)
                    step.done(ts(HIU[:, 1], SJU, 15, None, ALU.bitwise_and))
                    step.done(dve.tensor_copy(HIF, HIU))
                    tif = TIF.rearrange("p (h q) k -> p h q k", q=2)
                    for q in range(2):
                        i16 = I16.unsqueeze(1).to_broadcast([P, NH * TOPK, TOPK])
                        hf = HIF[:, q].rearrange("p h k -> p (h k)").unsqueeze(2)
                        step.done(tt(EQ.rearrange("p h k m -> p (h k) m"), i16, wide(hf, [P, NH * TOPK, TOPK]),
                                     ALU.is_equal))
                        step.done(tt(EQ, EQ, wide(tif[:, :, q, :].unsqueeze(2), [P, NH, TOPK, TOPK]), ALU.mult))
                        step.done(dve.tensor_reduce(GATE[:, 1 + q], EQ, AXX, ALU.add))
                    dve.wait_ge(S["gate_exp"], i + (base + 1))
                    step.done(dve.tensor_reduce(GSUM[:, 0], GATE[:, 0], AXX, ALU.add))
                    step.done(dve.reciprocal(GSUM[:, 1], GSUM[:, 0]))
                    tt(GATE[:, 0], GATE[:, 0], wide(GSUM[:, 1].unsqueeze(2), [P, NH, TOPK]), ALU.mult)\
                        .then_inc(S["gates_ready"], 1)
                    if l == 0:
                        m, count, pos = ADA_GROUPS[20]
                        dve.wait_ge(S["w_used"], i * count + (pos + count))
                        mm = bass.ds(i * count + m, count)
                        tt(M2[:, mm, :], ps[:, 5, 0:2 * count].rearrange("p (m z) -> p m z", z=2),
                           adab[:, mm].unsqueeze(2).to_broadcast([P, count, 2]), ALU.add).then_inc(S["ada_taken"], 1)
                    dve.wait_ge(S["slots_t"], i + (base + 1))
                step.leave(tiles, n0)

            def onehots(n, quarter, t0, g, i=0):
                toks = bass.ds(i * 4 * GTOK + (t0 + g * GTOK), GTOK)
                wait(dve, S["oh_used"], i * 4 + (n - 1))
                wait(dve, S["oh_ready"], i * 4 + (n - 1))
                keys = iota[:, quarter * QKEYS:(quarter + 1) * QKEYS]
                wide = [P, GTOK, QKEYS]
                tt(EQK[:, n % 2], keys.unsqueeze(1).to_broadcast(wide), SL[:, 1, toks].unsqueeze(2).to_broadcast(wide),
                   ALU.is_equal).then_inc(S["eq_ready"], 1)
                tt(OHB[:, n % 2], iota[:, :].unsqueeze(1).to_broadcast([P, GTOK, P]),
                   SL[:, 2, toks].unsqueeze(2).to_broadcast([P, GTOK, P]), ALU.is_equal)
                dve.wait_ge(S["eq_ready"], i * 4 + (n + 1))
                pair = [P, GTOK, 2, QKEYS]
                tt(OHA[:, n % 2], EQK[:, n % 2].unsqueeze(2).to_broadcast(pair),
                   GP[:, toks, :].unsqueeze(3).to_broadcast(pair), ALU.mult)\
                    .then_inc(S["oh_ready"], 1)

            def gates_in(n, buf, g, i=0):
                dve.wait_ge(S["g_high"], i * 4 + (n + 1))
                x = G[:, buf, :, bass.ds(i * 4 * GTOK + g * GTOK, GTOK)]
                tt(x, x, gate_sums(n)[:, 1], ALU.add).then_inc(S["g_taken"], 1)

            def first_quarter(n0, tiles, width):
                dve.wait_ge(S["slots_in"], tiles)
                wait(dve, S["oh_used"], n0)
                step.done(dve.tensor_copy(GRND[:, 0:width], SL[:, 0, 0:width]))
                dve.tensor_copy(GP[:, 0:width, 0], GRND[:, 0:width])
                step.done(tt(GP[:, 0:width, 1], SL[:, 0, 0:width], GRND[:, 0:width], ALU.subtract))
                for g in range(4):
                    onehots(n0 + g, 0, 0, g)
                    if g:
                        gates_in(n0 + g - 1, 0, g - 1)
                with dve.Fori(1, GROUPS // 4) as i:
                    for g in range(4):
                        onehots(n0 + g, 0, 0, g, i)
                        gates_in(n0 + g - 1, 0, g - 1, i)
                gates_in(n0 + GROUPS - 1, 0, GROUPS - 1)

            def low(p, k, i=0):
                n = AT_PEER[p] + k
                dve.wait_ge(S["hi_ready"], i * TURN + (p * N_PEER + k + 1))
                tt(WLO[:, k % 4].rearrange("p k n -> p (k n)"), wring[:, n % RING * TILE:(n % RING + 1) * TILE],
                   WHI[:, k % 4].rearrange("p k n -> p (k n)"), ALU.subtract).then_inc(S["w_used"], 1)

            def operands(p):
                t0 = PASS_TOK[p]
                for c in range(KD):
                    dve.wait_ge(S["xhi_ready"], KD * p + c + 1)
                    tt(XLO[:, c, :], A[:, c, t0:t0 + SEQ], XHI[:, c, :], ALU.subtract).then_inc(S["x_ready"], 1)
                for k in range(3):
                    low(p, k)

            def experts(p):
                m0, g0 = p * NKEY, PASS_GROUP[p]

                def turn(q, i, e0):
                    for m in range(e0, e0 + 4):
                        if p == 0 or q < QUARTERS - 1:
                            nq = (q + 1) % QUARTERS
                            onehots(g0 + m, nq, SEQ if p == 1 or nq == 0 else 0, m % QKEYS, i)
                        dve.wait_ge(S["gelu_done"], i * 4 + (m0 + m + 1))
                        tt(GL[:, m % 2, :], GL[:, m % 2, :],
                           G[:, q % 2, bass.ds(i * 4 + m % QKEYS, 1), :].rearrange("p e t -> p (e t)"), ALU.mult)\
                            .then_inc(S["mul_ready"], 1)
                        if m + 2 < NKEY:
                            low(p, tile_u(m + 2), i)
                        dve.wait_ge(S["acthi_ready"], i * 4 + (m0 + m + 1))
                        tt(ACL[:, m % 2, :], GL[:, m % 2, :], ACH[:, m % 2, :], ALU.subtract)\
                            .then_inc(S["act_ready"], 1)
                        if m + 1 < NKEY:
                            low(p, tile_v(m + 1), i)
                        if p == 0 or q < QUARTERS - 1:
                            gates_in(g0 + m, (q + 1) % 2, m % QKEYS, i)

                quarters(dve, turn, lambda q: dve.wait_ge(S["g_taken"], g0 + q * QKEYS))

            def peer_residual(p, l, s):
                def ready(c):
                    if c == 0:
                        dve.wait_ge(S["part_used"], (p + 1) * N_PEER)
                residual(l, 5, 0, lambda c, _: ps[:, 4 + c // 2, c % 2 * SEQ:(c % 2 + 1) * SEQ], SEQ, [s], ready)

            def forget():
                for m in range(16):
                    dve.wait_ge(S["hg_taken"], 8 + m + 1)
                    step.done(ts(LF[:, m, :], LF[:, m, :], lbs[:, 112 + m:113 + m], lbs[:, 96 + m:97 + m],
                                 ALU.mult, ALU.add))
                    d, h = m // 8, m % 8
                    ts(RKL[:, d, h, :], LF[:, m, 0:SEQ], -1.0, 1.0, ALU.mult, ALU.add)
                    ts(RKC[:, d, h, :], LF[:, m, SEQ:T], -1.0, 1.0, ALU.mult, ALU.add).then_inc(S["fk_done"], 1)
                dve.wait_ge(S["ln_done"], 1)
                dve.wait_ge(S["a_ready"], 3 * KD)
                one = hand[:, 0:SEQ]
                dve.memset(EL[:, :, :, 0:1], 0.0)
                dve.memset(EC[:, 1, :, 0:1], 0.0)
                step.done(dve.memset(one, 1.0))
                for h in range(NH):
                    dve.tensor_tensor_scan(EC[:, 0, h, :], one, LF[:, h, SEQ:T], 0.0, ALU.mult, ALU.add)
                    dve.tensor_tensor_scan(EC[:, 1, h, 1:SEQ], one[:, 0:SEQ - 1], LF[:, 8 + h, SEQ:T - 1], 0.0,
                                           ALU.mult, ALU.add)
                for m in range(16):
                    for d in range(2):
                        ins = dve.tensor_tensor_scan(EL[:, d, m, 1:129], one[:, 0:P],
                                                     LF[:, 8 * d + m // 2, m % 2 * P:(m % 2 + 1) * P], 0.0,
                                                     ALU.mult, ALU.add)
                ins.then_inc(S["scan_done"], 1)

            def states():
                dve.wait_ge(S["ck_exp"], 1)
                tt(CK[:, 0], CK[:, 0], RKC[:, 0], ALU.mult).then_inc(S["ck_ready"], 1)
                tt(CK[:, 1], CK[:, 1], RKC[:, 1], ALU.mult).then_inc(S["ck_ready"], 2)
                dve.wait_ge(S["lk_exp"], 1)
                tt(LK[:, 0], LK[:, 0], RKL[:, 0, :, 0:P], ALU.mult).then_inc(S["lk_ready"], 1)
                tt(LK[:, 1], LK[:, 1], RKL[:, 1, :, P:SEQ], ALU.mult).then_inc(S["lk_ready"], 1)
                dve.wait_ge(S["qi_exp"], 1)
                for d in range(2):
                    tt(QI[:, d], QI[:, d], RQ, ALU.mult).then_inc(S["qi_ready"], 1)
                dve.tensor_copy(lbs[:, 0:8], EL[:, 0, 0:16:2, 128])
                dve.tensor_copy(lbs[:, 8:16], EL[:, 1, 1:16:2, 128]).then_inc(S["dec_in"], 1)

            def carry():
                dve.wait_ge(S["dec_exp"], 1)
                for n in range(4):
                    d, hh = n // 2, n % 2
                    dve.wait_ge(S["ls_ready"], n + 1)
                    for h in range(4):
                        hd = 4 * hh + h
                        ins = stt(ST[:, 1, d, hd, :], ST[:, 0, d, hd, :], lbs[:, 16 + 8 * d + hd:17 + 8 * d + hd],
                                  ps[:, 4 + n, h * P:(h + 1) * P], ALU.mult, ALU.add)
                    ins.then_inc(S["ls_done"], 1)

            def levels():
                for lv in range(LEVELS + 1):
                    m = P >> (lv + 1)
                    q, k = LV[lv % 2]
                    if lv == 0:
                        dve.wait_ge(S["masks_in"], 16)
                        dve.wait_ge(S["ls_ready"], 4)
                    if lv >= 2:
                        dve.wait_ge(S["lv_prod"], 4 * (lv - 1))
                    if lv == LEVELS:
                        kv = k.rearrange("p (h t) n -> p h (t n)", h=NH)
                        qv = q.rearrange("p (h t) n -> p h (t n)", h=NH)
                        dve.tensor_copy(qv, RQ)
                        tt(kv, RKL[:, 0], RKL[:, 1], ALU.add).then_inc(S["lv_ready"], 1)
                    else:
                        seg = P // (2 * m)

                        def cut(x, off, lo):
                            y = x[:, :, off:off + P].rearrange("p m (s u) -> p m s u", s=seg)
                            return y[:, :, :, lo * m:lo * m + m]

                        def mid(x):
                            y = x[:, :, 0:P].rearrange("p m (s u) -> p m s u", s=seg)
                            return y[:, :, :, m:m + 1].to_broadcast([P, 16, seg, m])

                        def half(x, lo):
                            return x.rearrange("p m (s u) -> p m s u", s=seg)[:, :, :, lo * m:lo * m + m]

                        ef, eb = EL[:, 0], EL[:, 1]
                        tt(half(q, 1), cut(ef, 1, 1), mid(ef), ALU.subtract)
                        tt(half(q, 0), mid(eb), cut(eb, 0, 0), ALU.subtract)
                        tt(half(k, 0), mid(ef), cut(ef, 1, 0), ALU.subtract)
                        tt(half(k, 1), cut(eb, 0, 1), mid(eb), ALU.subtract).then_inc(S["lv_diff"], 1)
                        dve.wait_ge(S["lv_exp"], lv + 1)
                        qv = q.rearrange("p (h t) n -> p h (t n)", h=NH)
                        tt(qv, qv, RQ, ALU.mult)
                        kl = RKL.rearrange("p d h (t n) -> p d (h t) n", t=2)
                        tt(half(k, 0), half(k, 0), half(kl[:, 0], 0), ALU.mult)
                        tt(half(k, 1), half(k, 1), half(kl[:, 1], 1), ALU.mult).then_inc(S["lv_ready"], 1)
                    for b in range(4):
                        dve.wait_ge(S["lv_prod"], 4 * lv + b + 1)
                        dve.copy_predicated(AT_[:, 4 * b:4 * b + 4, :],
                                            masks[:, lv, :].unsqueeze(1).to_broadcast([P, 4, P]),
                                            ps[:, b, :].rearrange("p (m t) -> p m t", m=4)).then_inc(S["lv_taken"], 1)

            def readout():
                for b in range(4):
                    dve.wait_ge(S["ors_ready"], b + 1)
                    ts(ORS[:, 2 * b:2 * b + 2, :].rearrange("p h t -> p (h t)"), ps[:, b, :], 1.0 / P, EPS,
                       ALU.mult, ALU.add).then_inc(S["oms_ready"], 1)
                dve.wait_ge(S["ostd_ready"], 1)
                step.done(dve.reciprocal(ORS, ORS))
                for b in range(4):
                    o = ORS[:, 2 * b:2 * b + 2, :]
                    step.done(tt(o, ps[:, 4 + b, :].rearrange("p (h t) -> p h t", h=2), o, ALU.mult))
                    stt(MX1[:, 2 * b:2 * b + 2, :], o, ong[:, 0:1], RG[:, 2 * b:2 * b + 2, :], ALU.mult, ALU.mult)\
                        .then_inc(S["mx_ready"], 1)

            dve.wait_ge(S["consts_in"], 16 * len(first))
            bounds()
            filters()
            for g in range(4):
                ada(g)
            gains_of([0], 4)
            norm(0, T)
            for g in range(4, 20):
                ada(g)
            gains_of([1], 20)
            short_conv()
            hyena()
            rope()
            attention()
            residual(0, 2, 0, lambda c, s: ps[:, c % 4, s * SEQ:(s + 1) * SEQ], T, [0, 1],
                     lambda c: dve.wait_ge(S["w_used"], AT_ABOUT + c + 1))
            norm(1, T)
            routing(0, TT)
            gains_of([2, 3], 20 + TT)
            operands(0)
            first_quarter(0, TT, T)
            experts(0)
            peer_residual(0, 0, 0)
            operands(1)
            experts(1)
            peer_residual(1, 0, 1)
            norm(2, T)
            forget()
            states()
            carry()
            levels()
            readout()
            residual(1, 2, 0, lambda c, s: ps[:, c % 4, 0:SEQ], SEQ, [0],
                     lambda c: dve.wait_ge(S["w_used"], AT_HGOUT + c + 1))
            norm(3, SEQ)
            routing(1, CHUNKS)
            operands(2)
            first_quarter(2 * QUARTERS * GROUPS, TT + CHUNKS, SEQ)
            experts(2)
            peer_residual(2, 1, 0)
            norm(4, SEQ)


def tables():
    f32 = np.float32
    t = {"ident": np.eye(P, dtype=f32), "ones": np.ones((P, P), f32),
         "iota": np.tile(np.arange(P, dtype=f32), (P, 1))}
    f, n = np.arange(256)[:, None], np.arange(256)[None, :]
    ang = np.pi * (2 * f + 1) * n / 512.0
    cut = lambda m: m.reshape(2, P, 256).transpose(1, 0, 2).reshape(P, 512)
    t["dft"] = np.concatenate([cut(np.cos(ang).T), cut(np.sin(ang).T), cut(np.cos(ang) / 256), cut(np.sin(ang) / 256)],
                              axis=1).astype(f32)
    lin = np.linspace(0.0, 1.0, SEQ, dtype=f32)[:, None]
    w = (f32(2.0 * np.pi) * np.arange(SEQ, dtype=f32)[:, None] / f32(SEQ)).astype(f32)
    fr = np.linspace(1e-4, 15, 16, dtype=f32)[None, :]
    fw = (fr * w).astype(f32)
    t["zpos"] = np.concatenate([lin, np.cos(fw), -np.sin(fw)], axis=1).T.astype(f32)
    deltas = np.abs(np.linspace(np.log(1e-2) / 1.5, np.log(1e-2) / 0.3, HYC, dtype=f32))
    t["decay"] = np.exp(-lin * deltas).astype(f32).reshape(2, P, HYC).transpose(1, 0, 2).reshape(P, 1024)
    am = np.zeros((P, 2, 512), f32)
    q, k = np.arange(P)[:, None], np.arange(256)[None, :]
    for i in range(2):
        am[:, i, 0:256] = np.where(np.abs(q + i * P - k) <= 128, 0.0, -1.0e30)
    t["amask"] = am.reshape(P, 1024)
    inv = (10000.0 ** (-np.arange(16, dtype=f32) / 16)).astype(f32)
    pos = [np.repeat(np.arange(SEQ // 64), 64).astype(f32), np.tile(np.arange(64), SEQ // 64).astype(f32)]
    rope = np.zeros((P, 640), f32)
    for p in range(P):
        d = p % 64
        x = (pos[d // 32] * inv[d % 16]).astype(f32)
        rope[p, 0:256], rope[p, 256:512] = np.cos(x), np.sin(x)
        b = d % 32 >= 16
        rope[p - 16 if b else p + 16, 512 + p] = 1.0 if b else -1.0
    t["rope"] = rope
    s, u = np.arange(P)[:, None], np.arange(P)[None, :]
    m = [((s >> (6 - lv)) ^ (u >> (6 - lv))) == 1 for lv in range(7)] + [s == u]
    t["masks"] = np.concatenate(m, axis=1).astype(f32)
    return t


def tiles(w):
    n = w.shape[1]
    return np.ascontiguousarray(w.reshape(KD, P, n // P, P).transpose(2, 1, 0, 3)).reshape(n // P, P, TILE)


def columns(v):
    return np.asarray(v).reshape(-1, P).T


def layout(x, c, ctx, c_ctx, ada_w, ada_b, norm1_g, norm2_g, final_g, ab_w_in, ab_w_out,
           hy_conv_w, hy_conv_b, hy_filt_w1, hy_filt_b1, hy_filt_w2, hy_filt_b2, hy_filt_w3,
           hy_filt_freq, hy_skip, attn_sink, hg_w_in, hg_w_out, hg_lb_logits, hg_onorm_g,
           peer_wq, peer_keys, peer_u, peer_v):
    a = tables()
    xt = np.concatenate([x[0], ctx[0]], axis=0).T
    a["xT"] = xt.reshape(KD, P, T).transpose(1, 0, 2).reshape(P, KD * T)
    a["cc"] = np.stack([columns(c[0]), columns(c_ctx)], axis=2).reshape(P, 2 * KD)
    a["ada"] = np.concatenate([tiles(ada_w[l]) for l in range(2)])
    a["adab"] = np.concatenate([columns(ada_b[l]) for l in range(2)], axis=1)
    a["gains"] = np.concatenate([columns(g) for g in (norm1_g[0], norm2_g[0], norm1_g[1], norm2_g[1], final_g)], axis=1)
    order = np.concatenate([np.arange(h * HD, (h + 1) * HD) for c in range(4) for h in (c, c + 4)])
    win = np.concatenate([ab_w_in[0][:, :1536], ab_w_in[0][:, 1536 + order], ab_w_in[0][:, 2048:]], axis=1)
    a["abin"] = tiles(win)
    a["about"] = tiles(np.concatenate([ab_w_out[0][:512], ab_w_out[0][512 + order]], axis=0))
    a["conv"] = np.concatenate([columns(hy_conv_w[0][n]) for n in range(3)] + [columns(hy_conv_b[0])], axis=1)
    a["dskip"] = np.concatenate([columns(hy_skip[0][n]) for n in range(2)], axis=1)
    a["sink"] = np.tile(attn_sink[0][None, :], (P, 1))
    a["fw1"], a["fw2"], a["fw3"] = hy_filt_w1[0], hy_filt_w2[0], hy_filt_w3[0]
    a["fvec"] = np.stack([hy_filt_b1[0], hy_filt_b2[0], hy_filt_freq[0]], axis=1)
    a["lbl"] = np.concatenate([columns(hg_lb_logits[n].reshape(-1)) for n in range(2)], axis=1)
    a["ong"] = hg_onorm_g[0][:, None]
    a["hgin"], a["hgout"] = tiles(hg_w_in[0]), tiles(hg_w_out[0])
    for l in range(2):
        a[f"wq{l}"] = tiles(peer_wq[l])
        a[f"keys{l}"] = peer_keys[l].reshape(16, NKEY, P).transpose(2, 0, 1).reshape(P, 16 * NKEY)
        a[f"u{l}"] = np.ascontiguousarray(peer_u[l].reshape(NKEY, NKEY, KD, P).transpose(0, 3, 2, 1))\
            .reshape(NKEY, P, TILE)
        a[f"v{l}"] = peer_v[l].reshape(NKEY, NKEY, D)
    return {k: np.ascontiguousarray(v) for k, v in a.items()}


def kernel(**inputs):
    import concourse.bacc as bacc
    from concourse.bass_utils import run_bass_kernel_spmd

    arrays = layout(**{k: np.asarray(v) for k, v in inputs.items()})
    nc = bacc.Bacc("TRN2", target_bir_lowering=False, num_devices=1)
    aps = {k: nc.dram_tensor(f"in_{k}", v.shape, mybir.dt.from_np(v.dtype), kind="ExternalInput").ap()
           for k, v in arrays.items()}
    out = nc.dram_tensor("out_t", (P, KD, SEQ), F32, kind="ExternalOutput").ap()
    build(nc, aps, out)
    r = run_bass_kernel_spmd(nc, [{f"in_{k}": v for k, v in arrays.items()}], core_ids=[0])
    got = np.asarray(r.results[0]["out_t"]).reshape(P, KD, SEQ)
    return np.ascontiguousarray(got.transpose(2, 1, 0).reshape(1, SEQ, D))
```

```python
from contextlib import ExitStack

import numpy as np

import concourse.bass as bass
from concourse import mybir

F32 = mybir.dt.float32
F32R = mybir.dt.float32r
BF16 = mybir.dt.bfloat16
U32 = mybir.dt.uint32
ALU = mybir.AluOpType
ACT = mybir.ActivationFunctionType
AXX = mybir.AxisListType.X

P = 128
D = 1024
KD = D // P
SEQ = 256
T = 2 * SEQ
TT = T // P
NMOD = 6
EPS = 1e-6
HYC = 512
HC = HYC // P
NQ = 8
HD = 64
NH = 8
TOPK = 16
NKEY = 128
CHUNKS = SEQ // P
LEVELS = 7
RING = 4
TURN = 8
TILE = KD * P
NEG = -3.0e38
ARENA = 34048
TWO_PI = 2.0 * np.pi
PI_A = 6.28125
PI_B = float(np.float32(TWO_PI - PI_A) // np.float32(2.0 ** -20) * 2.0 ** -20)
PI_C = float(np.float32(TWO_PI - PI_A - PI_B))
ROUND = 12582912.0

N_ADA = 2 * NMOD * KD
ADA_FIRST = 2 * KD
ADA_AB = 2
AB_GROUPS = 12
ADA_ROUTE = (N_ADA - ADA_FIRST - AB_GROUPS * ADA_AB) // TT
N_ABIN, N_OUT, N_WQ, N_HGIN, N_PEER = 18, KD, 16, 40, 2 * NKEY
AT_ADA = 0
AT_ABIN = AT_ADA + ADA_FIRST
AT_ABOUT = AT_ABIN + N_ABIN + AB_GROUPS * ADA_AB
AT_WQ0 = AT_ABOUT + N_OUT
AT_ROUTE = AT_WQ0 + N_WQ
AT_PEER = [AT_ROUTE + TT * ADA_ROUTE, AT_ROUTE + TT * ADA_ROUTE + N_PEER, 0]
AT_HGIN = AT_PEER[1] + N_PEER
AT_HGOUT = AT_HGIN + N_HGIN
AT_WQ1 = AT_HGOUT + N_OUT
AT_PEER[2] = AT_WQ1 + N_WQ


def at_abin(j):
    return AT_ABIN + j + ADA_AB * min(j, AB_GROUPS)


ADA_GROUPS = ([(4 * g, 4, AT_ADA + 4 * g) for g in range(ADA_FIRST // 4)]
              + [(ADA_FIRST + ADA_AB * j, ADA_AB, at_abin(j) + 1) for j in range(AB_GROUPS)]
              + [(ADA_FIRST + AB_GROUPS * ADA_AB + ADA_ROUTE * j, ADA_ROUTE, AT_ROUTE + ADA_ROUTE * j) for j in range(TT)])
FIRST_GROUPS = ADA_FIRST // 4
ROUTE_GROUP = FIRST_GROUPS + AB_GROUPS
ROUTE_STEPS = 19

HG_SPLIT = 24

QKEYS = 32
GTOK = 8
GROUPS = SEQ // GTOK
QUARTERS = NKEY // QKEYS
PASS_GROUP = [GROUPS, 5 * GROUPS, 9 * GROUPS]
PASS_TOK = [0, SEQ, 0]


def tile_u(m):
    return 2 * m - 1 if m else 0


def tile_v(m):
    return min(2 * m + 2, N_PEER - 1)


def wait(eng, sem, value):
    if isinstance(value, int) and value <= 0:
        return
    eng.wait_ge(sem, value)


class Chain:

    def __init__(self, eng, sem, settle):
        self.settle = settle
        self.eng, self.sem, self.n, self.i, self.per = eng, sem, 0, None, 0

    def at(self, n):
        return n if self.i is None else self.i * self.per + n

    def done(self, ins):
        self.n += 1
        ins.then_inc(self.sem, 1)
        self.eng.wait_ge(self.sem, self.at(self.n))
        if self.i is not None:
            self.settle()

    def enter(self, i, per):
        self.i, self.per = i, per

    def leave(self, trips, n0):
        assert self.n - n0 == self.per, (self.n - n0, self.per)
        self.n = n0 + trips * self.per
        self.i = None


def build(nc, a, out):
    with ExitStack() as ctx:
        def sb(name, words, dt=F32):
            return ctx.enter_context(nc.sbuf_tensor(name, [P, words], dt))

        def sem(name):
            return ctx.enter_context(nc.semaphore(name))

        arena_at = -(-nc.sbuf_base // 32) * 32
        arena = sb("arena", ARENA)
        h_t = sb("h_t", KD * T)
        a_t = sb("a_t", KD * T)
        wring = sb("wring", RING * TILE)
        hand = sb("hand", 1024)
        slots = sb("slots", 3 * T)
        ident = sb("ident", P)
        ones = sb("ones", P)
        iota = sb("iota", P)
        mods = sb("mods", 2 * NMOD * KD * 2)
        gmod = sb("gmod", 4 * KD * 2)
        gains = sb("gains", 5 * KD)
        csil = sb("csil", KD * 2)
        adab = sb("adab", 2 * NMOD * KD)
        conv = sb("conv", 4 * 12)
        dskip = sb("dskip", 2 * HC)
        sinks = sb("sinks", 2 * NQ)
        lbs = sb("lbs", 8 * 16)
        ong = sb("ong", 1)
        filt = sb("filt", 4)
        small = sb("small", 16)
        tick = sb("tick", 1)
        ps = ctx.enter_context(nc.psum_tensor("ps", [P, 8, 512], F32))

        H = h_t[:, :].rearrange("p (k t) -> p k t", k=KD)
        A = a_t[:, :].rearrange("p (k t) -> p k t", k=KD)
        W = wring[:, :].rearrange("p (r k n) -> p r k n", r=RING, k=KD)
        M = mods[:, :].rearrange("p (l s c z) -> p l s c z", l=2, s=NMOD, c=KD)
        M2 = mods[:, :].rearrange("p (m z) -> p m z", z=2)
        GM = gmod[:, :].rearrange("p (n c z) -> p n c z", n=4, c=KD)
        GN = gains[:, :].rearrange("p (n c) -> p n c", n=5)
        CS = csil[:, :].rearrange("p (k z) -> p k z", z=2)
        rstd = hand[:, 0:T]
        SL = slots[:, :].rearrange("p (q t) -> p q t", q=3)

        def over(name, at, count, dt=F32R):
            return nc.alloc_sbuf_tensor_at(name, [P, count], dt, offset=arena_at + 4 * at)

        def view(at, pattern=None, **kw):
            n = 1
            for v in kw.values():
                n *= v
            x = arena[:, at:at + n]
            return x.rearrange(pattern, **kw) if pattern else x

        COSF = view(0, "p (c f) -> p c f", c=2, f=256)
        SINF = view(512, "p (c f) -> p c f", c=2, f=256)
        COSG = view(1024, "p (c t) -> p c t", c=2, t=256)
        SING = view(1536, "p (c t) -> p c t", c=2, t=256)
        HF = view(2048, "p (o q f c) -> p o q f c", o=2, q=2, f=2, c=512)
        HRAW = view(6144, "p (t o d c) -> p t o d c", t=2, o=2, d=2, c=512)
        HABS = view(10240, "p (t o d c) -> p t o d c", t=2, o=2, d=2, c=512)
        HSUM = view(14336, "p (o t c) -> p o t c", o=2, t=2, c=512)
        HDIF = view(16384, "p (o t c) -> p o t c", o=2, t=2, c=512)
        RNRM = view(18432, "p (o c) -> p o c", o=2, c=512)
        FW3 = arena[0:64, 19456:21504]
        ZPOS = arena[0:33, 21504:21760]
        FARG = arena[0:64, 21760:22016]
        FRND = arena[0:64, 22016:22272]
        FHID = [arena[0:64, 22272:22528], arena[0:64, 22528:22784]]
        DECAY = view(22784, "p (t c) -> p t c", t=2, c=512)
        FW1 = arena[0:33, 23808:23872]
        FW2 = arena[0:64, 23872:23936]
        U = view(6144, "p (j t) -> p j t", j=12, t=T)
        UC = view(12288, "p (j t) -> p j t", j=12, t=T)
        ZT = view(18432, "p (t c) -> p t c", t=TT, c=512)
        PF = view(20480, "p (s q f c) -> p s q f c", s=2, q=2, f=2, c=512)
        QT = view(24576, "p (j t) -> p j t", j=4, t=T)
        KT = arena[:, 26624:27136]
        VT = view(27136, "p (t n) -> p t n", t=TT, n=P)
        Z1 = view(27648, "p (c t) -> p c t", c=HC, t=T)
        AMASK = view(29696, "p (i k) -> p i k", i=2, k=512)
        ROPE = view(30720, "p (q t) -> p q t", q=2, t=SEQ)
        ROT = arena[:, 31232:31360]
        RTMP = arena[:, 31360:31872]
        MIX = U
        SQ = view(24576, "p (k t) -> p k t", k=KD, t=T)
        ASC = view(18432, "p (b n) -> p b n", b=2, n=512)
        APR = view(19456, "p (b n) -> p b n", b=2, n=512)
        APT = view(20480, "p (b k q) -> p b k q", b=2, k=4, q=P)
        CVT = view(29696 - 2048, "p (c t) -> p c t", c=4, t=T)

        PQT = view(0, "p (j t) -> p j t", j=16, t=T)
        KEYS = view(8192, "p (j n) -> p j n", j=16, n=NKEY)
        PQC = view(10240, "p (j t) -> p j t", j=16, t=P)
        PS1 = view(12288, "p (j n) -> p j n", j=16, n=NKEY)
        PS2 = view(14336, "p (j n) -> p j n", j=16, n=NKEY)
        CAND = view(16384, "p (h n) -> p h n", h=NH, n=256)
        CAN2 = view(18432, "p (h n) -> p h n", h=NH, n=256)
        EQ = view(20480, "p (h k m) -> p h k m", h=NH, k=TOPK, m=TOPK)
        TV = view(22528, "p (j k) -> p j k", j=16, k=TOPK)
        TIU = view(22784, "p (j k) -> p j k", j=16, k=TOPK).bitcast(U32)
        TIF = view(23040, "p (j k) -> p j k", j=16, k=TOPK)
        SV = view(23296, "p (h k) -> p h k", h=NH, k=TOPK)
        SJU = view(23424, "p (h k) -> p h k", h=NH, k=TOPK).bitcast(U32)
        HIU = view(23552, "p (q h k) -> p q h k", q=2, h=NH, k=TOPK).bitcast(U32)
        HIF = view(23808, "p (q h k) -> p q h k", q=2, h=NH, k=TOPK)
        GATE = view(24064, "p (q h k) -> p q h k", q=3, h=NH, k=TOPK)
        GSUM = view(24448, "p (q h) -> p q h", q=2, h=NH)
        G = view(0, "p (b e t) -> p b e t", b=2, e=QKEYS, t=SEQ)
        WHI, WLO = [over(n, at, 4 * TILE)[:, :].rearrange("p (r k n) -> p r k n", r=4, k=KD)
                    for n, at in (("w_hi", 16384), ("w_lo", 20480))]
        XHI, XLO = [over(n, at, KD * SEQ)[:, :].rearrange("p (k t) -> p k t", k=KD)
                    for n, at in (("x_hi", 24576), ("x_lo", 26624))]
        OHB = over("second_onehot", 28672, 2 * P * GTOK, BF16)[:, :].rearrange("p (g e u) -> p g e u", g=2, u=GTOK)
        OHA = over("gated_onehot", 29696, 6 * QKEYS * GTOK, BF16)[:, :]\
            .rearrange("p (g q e u) -> p g q e u", g=2, q=3, u=GTOK)
        EQK = over("first_onehot", 30464, 2 * QKEYS * GTOK, BF16)[:, :].rearrange("p (g e u) -> p g e u", g=2, u=GTOK)
        KEYNUM = over("key_numbers", 30720, P * GTOK, BF16)[:, :].rearrange("p (e u) -> p e u", u=GTOK)
        KEY12 = over("slot_keys", 31232, 2 * T, BF16)[:, :].rearrange("p (q t) -> p q t", q=2)
        GP = over("gate_parts", 31744, 3 * T, BF16)[:, :].rearrange("p (q t) -> p q t", q=3)
        GREST = view(32512, None, t=T)
        GL = view(32512, "p (r t) -> p r t", r=2, t=SEQ)
        ACH, ACL = [over(n, at, 2 * SEQ)[:, :].rearrange("p (r t) -> p r t", r=2)
                    for n, at in (("act_hi", 33024), ("act_lo", 33536))]
        I16 = iota[:, 0:TOPK]

        def weight_parts(name, hi, lo, ring):
            return [over(name + x, at, ring * TILE)[:, :].rearrange("p (r k n) -> p r k n", r=ring, k=KD)
                    for x, at in (("_w_hi", hi), ("_w_lo", lo))]

        A_HI, A_LO_Q, A_LO_G = [over(n, at, KD * T)[:, :].rearrange("p (k t) -> p k t", k=KD)
                                for n, at in (("a_hi", 28672), ("a_lo_q", 10240), ("a_lo_g", 24576))]
        wq_parts = weight_parts("wq", 14336, 18432, 4)
        hg_parts = weight_parts("hg", 20480, 22528, 2)
        SPLIT = {"wq0": (AT_WQ0, N_WQ, 0, 1, T, 4, wq_parts, A_LO_Q),
                 "hg": (AT_HGIN, HG_SPLIT, N_WQ, 2, T, 2, hg_parts, A_LO_G),
                 "wq1": (AT_WQ1, N_WQ, N_WQ + HG_SPLIT, 3, SEQ, 4, wq_parts, A_LO_Q)}

        RQ = view(0, "p (h t) -> p h t", h=NH, t=SEQ)
        RG = view(2048, "p (h t) -> p h t", h=NH, t=SEQ)
        RKL = view(4096, "p (d h t) -> p d h t", d=2, h=NH, t=SEQ)
        RKC = view(8192, "p (d h t) -> p d h t", d=2, h=NH, t=SEQ)
        LF = view(12288, "p (m t) -> p m t", m=16, t=T)
        IV = view(20480, "p (t h n) -> p t h n", t=TT, h=NH, n=P)
        EL = view(24576, "p (d m t) -> p d m t", d=2, m=16, t=129)
        EC = view(28704, "p (d h t) -> p d h t", d=2, h=NH, t=SEQ)
        CK = view(12288, "p (d h t) -> p d h t", d=2, h=NH, t=SEQ)
        CKT = view(16384, "p (t d h n) -> p t d h n", t=2, d=2, h=NH, n=P)
        LK = view(12288, "p (d h t) -> p d h t", d=2, h=NH, t=P)
        LKT = view(14336, "p (d h n) -> p d h n", d=2, h=NH, n=P)
        ST = a_t[:, 0:4096].rearrange("p (z d h n) -> p z d h n", z=2, d=2, h=NH)
        QI = view(8192, "p (d h t) -> p d h t", d=2, h=NH, t=SEQ)
        LV = [[view(12288 + 4096 * b + 2048 * q, "p (m t) -> p m t", m=16, t=P) for q in range(2)] for b in range(2)]
        AT_ = view(28704, "p (m t) -> p m t", m=16, t=P)
        masks = view(30752, "p (l t) -> p l t", l=8, t=P).bitcast(U32)
        MX1 = view(30752, "p (h t) -> p h t", h=NH, t=SEQ)
        OSQ = view(12288, "p (h t) -> p h t", h=NH, t=SEQ)
        ORS = view(14336, "p (h t) -> p h t", h=NH, t=SEQ)

        names = """c_in consts_in arena_in keys_in masks_in x_in out_done w_used
            c_ready ada_taken mods_ready
            f_proj f_arg f_sin f_raw f_rawtaken f_abs f_norm f_parts f_spec f_spectaken
            sq_ready norm_summed ms_ready std_ready hn_ready a_ready
            ab_taken cv_mid cv_done
            zt_ready zt_taken zf_ready pf_ready yt_ready z_ready
            rot_ready rope_done
            sc_ready sc_taken nmax_ready exp_ready pn_ready pt_ready pt_taken pv_done att_done
            h_ready dec_in dec_exp
            wq_taken qc_ready route_scores scores_ready scores_used diff_ready gate_exp gates_ready
            slots_t slots_in
            a_hi_ready a_parts_ready w_hi_ready product_ready
            eq_ready oh_ready oh_used g_high g_taken
            xhi_ready x_ready hi_ready part_used gelu_done mul_ready acthi_ready act_ready
            hg_taken fk_done ln_done scan_done
            ck_exp ck_ready ck_t ck_in cs_ready cs_taken
            lk_exp lk_ready lk_t lk_in ls_ready ls_done
            qi_exp qi_ready lv_diff lv_exp lv_ready lv_prod lv_taken
            oi_ready osq_ready ors_ready oms_ready ostd_ready mx_ready
            f_in dve_step lb_diff lb_exp""".split()
        S = {n: sem(n) for n in names}
        w_loaded = [sem(f"w_loaded{r}") for r in range(RING)]
        block = ctx.enter_context(nc.Block())

        def settle_dve():
            nc.vector.tensor_copy(tick[:, 0:1], ones[:, 0:1])

        def parts(hi, lo, x_hi, x_lo):
            return [(hi, x_hi), (hi, x_lo), (lo, x_hi)]

        def gate_sums(n):
            return ps[:, 2 + n % 2, :].rearrange("p (t q e) -> p q e t", t=GTOK, q=2)

        def landed(eng, n, i=0):
            eng.wait_ge(w_loaded[n % RING], i * (16 * TURN // RING) + 16 * (n // RING + 1))

        def quarters(eng, turn, ready=lambda q: None):
            for q in range(QUARTERS):
                ready(q)
                e0, first_turn, last_turn = q * QKEYS, int(q == 0), QKEYS // 4 - int(q == QUARTERS - 1)
                if first_turn:
                    turn(q, 0, 0)
                with eng.Fori(first_turn, last_turn) as i:
                    turn(q, i, e0)
            turn(QUARTERS - 1, 0, NKEY - 4)

        first = [(ident[:, :], a["ident"]), (ones[:, :], a["ones"]), (iota[:, :], a["iota"]),
                 (adab[:, :], a["adab"]), (gains[:, :], a["gains"]), (conv[:, :], a["conv"]),
                 (dskip[:, :], a["dskip"]), (sinks[:, 0:NQ], a["sink"]), (lbs[:, 0:32], a["lbl"]),
                 (ong[:, :], a["ong"])]
        filters_in = [(ZPOS, a["zpos"]), (FW1, a["fw1"]), (filt[0:64, 0:3], a["fvec"]), (FW2, a["fw2"]),
                      (FW3, a["fw3"]), (arena[:, 22784:23808], a["decay"]), (arena[:, 0:2048], a["dft"])]
        arena_loads = [(arena[:, 29696:30720], a["amask"]), (arena[:, 30720:31360], a["rope"])]

        @block.sync
        def _(sp):
            sp.dma_start(csil[:, :], a["cc"]).then_inc(S["c_in"], 16)

            def load(n, src, i=0):
                wait(sp, S["w_used"], i * TURN + (n - RING + 1))
                sp.dma_start(wring[:, n % RING * TILE:(n % RING + 1) * TILE], src).then_inc(w_loaded[n % RING], 16)

            def row(src, x):
                return src[bass.ds(x, 1), :, :].rearrange("a p n -> p (a n)") if not isinstance(x, int) else src[x]

            def stream(n0, src, count, r0=0):
                turns = count // TURN
                for j in range(TURN):
                    load(n0 + j, row(src, r0 + j))
                if turns > 1:
                    with sp.Fori(1, turns) as i:
                        for j in range(TURN):
                            load(n0 + j, row(src, i * TURN + (r0 + j)), i)
                for j in range(turns * TURN, count):
                    load(n0 + j, row(src, r0 + j))

            def stream_with(at, src, count, groups):
                for j in range(count):
                    load(at(j), src[j])
                    if j < len(groups):
                        m, k, pos = groups[j]
                        for x in range(k):
                            load(pos + x, a["ada"][m + x])

            def experts(n0, u, v):
                def pairs(i, js):
                    for j in js:
                        load(n0 + 1 + 2 * j, row(u, i * 4 + (j + 1)), i)
                        load(n0 + 2 + 2 * j, row(v, i * 4 + j), i)

                load(n0, row(u, 0))
                pairs(0, range(4))
                with sp.Fori(1, NKEY // 4 - 1) as i:
                    pairs(i, range(4))
                last = NKEY - 4
                for e in range(last, NKEY):
                    if e + 1 < NKEY:
                        load(n0 + 1 + 2 * e, u[e + 1])
                    load(n0 + (2 + 2 * e if e + 1 < NKEY else 1 + 2 * e), v[e])

            stream(AT_ADA, a["ada"], ADA_FIRST)
            sp.dma_start(h_t[:, :], a["xT"]).then_inc(S["x_in"], 16)
            stream_with(at_abin, a["abin"], N_ABIN, ADA_GROUPS[FIRST_GROUPS:ROUTE_GROUP])
            stream(AT_ABOUT, a["about"], N_OUT)
            stream(AT_WQ0, a["wq0"], N_WQ)
            stream(AT_ROUTE, a["ada"], TT * ADA_ROUTE, ADA_FIRST + AB_GROUPS * ADA_AB)
            experts(AT_PEER[0], a["u0"], a["v0"])
            experts(AT_PEER[1], a["u0"], a["v0"])
            stream(AT_HGIN, a["hgin"], N_HGIN)
            stream(AT_HGOUT, a["hgout"], N_OUT)
            stream(AT_WQ1, a["wq1"], N_WQ)
            experts(AT_PEER[2], a["u1"], a["v1"])
            sp.wait_ge(S["a_ready"], 5 * KD)
            sp.dma_start(out, A[:, :, 0:SEQ]).then_inc(S["out_done"], 16)
            sp.wait_ge(S["out_done"], 16)

        @block.gpsimd
        def _(pool):
            for dst, src in first:
                pool.dma_start(dst, src).then_inc(S["consts_in"], 16)
            pool.wait_ge(S["w_used"], AT_ABOUT + N_OUT)
            pool.dma_start(arena[:, 8192:10240], a["keys0"]).then_inc(S["keys_in"], 16)

            pool.wait_ge(S["ck_exp"], 1)
            pool.dma_start(arena[:, 30752:31776], a["masks"]).then_inc(S["masks_in"], 16)
            pool.wait_ge(S["w_used"], AT_HGOUT + N_OUT)
            pool.dma_start(arena[:, 8192:10240], a["keys1"]).then_inc(S["keys_in"], 16)

        @block.tensor
        def _(pe):
            def group(o, pairs, sem=None, **kw):
                for n, (l, r) in enumerate(pairs):
                    ins = pe.matmul(o, l, r, start=n == 0, stop=n == len(pairs) - 1, **kw)
                if sem is not None:
                    ins.then_inc(S[sem], 1)
                return ins

            def filters():
                pe.wait_ge(S["f_in"], 16 * len(filters_in))
                pe.wait_ge(S["consts_in"], 16 * len(first))
                group(ps[0:64, 0, 0:256], [(FW1, ZPOS)], "f_proj")
                ada(2)
                pe.wait_ge(S["f_sin"], 1)
                group(ps[0:64, 1, 0:256], [(FW2, FHID[0])], "f_proj")
                ada(3)
                pe.wait_ge(S["f_sin"], 2)
                pe.wait_ge(S["ada_taken"], 4)
                for n in range(8):
                    wait(pe, S["f_rawtaken"], n - 1)
                    t, od = n // 4, n % 4
                    group(ps[:, 2 + n % 2, :], [(FHID[1][:, t * P:(t + 1) * P], FW3[:, od * 512:(od + 1) * 512])],
                          "f_raw")
                pe.wait_ge(S["f_abs"], 2)
                for o in range(2):
                    group(ps[:, 4 + o, :], [(ones[:, :], HABS[:, t, o, d, :]) for t in range(2) for d in range(2)],
                          "f_norm")
                pe.wait_ge(S["f_parts"], 1)
                for n in range(8):
                    o, q, f = n // 4, n // 2 % 2, n % 2
                    wait(pe, S["f_spectaken"], n - 1)
                    src, mat = (HSUM, COSF) if q == 0 else (HDIF, SINF)
                    group(ps[:, 6 + n % 2, :], [(mat[:, t, f * P:(f + 1) * P], src[:, o, t, :]) for t in range(2)],
                          "f_spec")

            def ada(g):
                m, count, pos = ADA_GROUPS[g]
                if g == 0:
                    pe.wait_ge(S["c_ready"], 1)
                wait(pe, S["ada_taken"], g - 1 if g < ROUTE_GROUP else g)
                for j in range(count):
                    n = pos + j
                    landed(pe, n)
                    group(ps[:, 5 + g % 2 if g < ROUTE_GROUP else 5, 2 * j:2 * j + 2],
                          [(W[:, n % RING, k, :], CS[:, k, :]) for k in range(KD)], "w_used")

            def norm(k, width):
                for c in range(KD):
                    pe.wait_ge(S["sq_ready"], KD * k + c + 1)
                    ins = pe.matmul(ps[:, 7, 0:width], ones[:, :], SQ[:, c, 0:width], start=c == 0, stop=c == KD - 1)
                ins.then_inc(S["norm_summed"], 1)

            def ab_in():
                pe.wait_ge(S["a_ready"], KD)
                for j in range(N_ABIN):
                    n = at_abin(j)
                    wait(pe, S["ab_taken"], j - 3)
                    landed(pe, n)
                    o = ps[:, j % 4, :]
                    if j < 17:
                        group(o, [(W[:, n % RING, k, :], A[:, k, :]) for k in range(KD)], "w_used")
                    else:
                        for t in range(TT):
                            ins = group(o[:, t * P:(t + 1) * P],
                                        [(A[:, k, t * P:(t + 1) * P], W[:, n % RING, k, :]) for k in range(KD)])
                        ins.then_inc(S["w_used"], 1)
                    if j < AB_GROUPS:
                        ada(FIRST_GROUPS + j)

            def hyena():
                pe.wait_ge(S["ab_taken"], N_ABIN)
                for o in range(2):
                    z = UC if o == 0 else Z1
                    pe.wait_ge(S["cv_done"] if o == 0 else S["z_ready"], 1 if o == 0 else HC)
                    for t in range(TT):
                        for c in range(HC):
                            ins = pe.transpose(ps[:, t, c * P:(c + 1) * P], z[:, c, t * P:(t + 1) * P], ident[:, :])
                        ins.then_inc(S["zt_ready"], 1)
                    for n in range(4):
                        s, f = n // 2, n % 2
                        pe.wait_ge(S["zt_taken"], TT * o + 2 * (s + 1))
                        if n >= 2:
                            pe.wait_ge(S["pf_ready"], 4 * o + n - 1)
                        for q, mat in enumerate((COSF, SINF)):
                            ins = group(ps[:, 4 + 2 * (n % 2) + q, :],
                                        [(mat[:, t, f * P:(f + 1) * P], ZT[:, 2 * s + t, :]) for t in range(2)])
                        ins.then_inc(S["zf_ready"], 1)
                    pe.wait_ge(S["pf_ready"], 4 * (o + 1))
                    for c in range(HC):
                        for s in range(2):
                            ins = group(ps[:, c, s * SEQ:(s + 1) * SEQ],
                                        [(PF[:, s, q, f, c * P:(c + 1) * P], (COSG, SING)[q][:, f, :])
                                         for f in range(2) for q in range(2)])
                        ins.then_inc(S["yt_ready"], 1)

            def rope():
                pe.wait_ge(S["arena_in"], 16 * len(arena_loads))
                for j in range(5):
                    wait(pe, S["rope_done"], j - 1)
                    pe.matmul(ps[:, 4 + j % 2, 0:SEQ], ROT, QT[:, j, 0:SEQ] if j < 4 else KT[:, 0:SEQ],
                              start=True, stop=True).then_inc(S["rot_ready"], 1)

            def attention():
                pe.wait_ge(S["rope_done"], 5)
                pe.wait_ge(S["z_ready"], 2 * HC)

                def scores(u):
                    c, g, i = u // 8, u // 4 % 2, u % 4
                    wait(pe, S["sc_taken"], u - 1)
                    keys = KT[64 * g:64 * g + 64, :] if i < 2 else KT[64 * g:64 * g + 64, SEQ:T]
                    pe.matmul(ps[:, u % 2, 0:512 if i < 2 else 256], QT[64 * g:64 * g + 64, c, i * P:(i + 1) * P],
                              keys, start=True, stop=True).then_inc(S["sc_ready"], 1)

                def turn(u):
                    i = u % 4
                    pe.wait_ge(S["pn_ready"], u + 1)
                    wait(pe, S["pt_taken"], u - 1)
                    for k in range(4 if i < 2 else 2):
                        ins = pe.transpose(ps[:, 2 + u % 2, k * P:(k + 1) * P], APR[:, u % 2, k * P:(k + 1) * P],
                                           ident[:, :])
                    ins.then_inc(S["pt_ready"], 1)

                def values(u):
                    c, g, i = u // 8, u // 4 % 2, u % 4
                    pe.wait_ge(S["pt_taken"], u + 1)
                    if u % 8 == 0:
                        wait(pe, S["att_done"], c - 1)
                    k0, kn = (0, 4) if i < 2 else (2, 2)
                    group(ps[64 * g:64 * g + 64, 4 + c % 2, i * P:(i + 1) * P],
                          [(VT[:, k0 + k, 64 * g:64 * g + 64], APT[:, u % 2, k, :]) for k in range(kn)], "pv_done")

                scores(0)
                for u in range(34):
                    if u + 1 < 32:
                        scores(u + 1)
                    if 1 <= u < 33:
                        turn(u - 1)
                    if u >= 2:
                        values(u - 2)

            def product(name, j, o, width):
                n0, count, m0, k, _, ring, (w_hi, w_lo), a_lo = SPLIT[name]
                pe.wait_ge(S["w_used"], n0 + j + 1)
                for c in range(KD):
                    if j == 0:
                        pe.wait_ge(S["a_parts_ready"], KD * (k - 1) + c + 1)
                    for n, (w, x) in enumerate(parts(w_hi[:, j % ring, c, :], w_lo[:, j % ring, c, :],
                                                     A_HI[:, c, 0:width], a_lo[:, c, 0:width])):
                        ins = pe.matmul(o, w, x, start=c == 0 and n == 0, stop=c == KD - 1 and n == 2)
                ins.then_inc(S["product_ready"], 1)

            def mixer_out(l, n0, src, width):
                for c in range(KD):
                    n = n0 + c
                    wait(pe, S["h_ready"], (0, 3 * KD)[l] + c - 3 if c >= 4 else 0)
                    landed(pe, n)
                    group(ps[:, c % 4, 0:width], [(W[:, n % RING, k, :], src[:, k, :]) for k in range(KD)], "w_used")

            def queries(l, width):
                for j in range(N_WQ):
                    wait(pe, S["wq_taken"], N_WQ * l + j - 3 if j >= 4 else 0)
                    product(f"wq{l}", j, ps[:, j % 4, 0:width], width)

            def routing(l, tiles):
                pe.wait_ge(S["keys_in"], 16 * (l + 1))
                base = (0, TT)[l]

                def scores(i):
                    pe.wait_ge(S["qc_ready"], base + i + 1)
                    for j in range(16):
                        ins = pe.matmul(ps[:, j // 4, j % 4 * P:(j % 4 + 1) * P], PQC[:, j, :], KEYS[:, j, :],
                                        start=True, stop=True)
                    ins.then_inc(S["route_scores"], 1)

                scores(0)
                for i in range(tiles):
                    if l == 0:
                        ada(ROUTE_GROUP + i)
                    if i + 1 < tiles:
                        scores(i + 1)
                    pe.wait_ge(S["gates_ready"], base + i + 1)
                    for q in range(3):
                        ins = pe.transpose(ps[:, 4, q * P:(q + 1) * P],
                                           GATE[:, q, :, :].rearrange("p h k -> p (h k)"), ident[:, :])
                    ins.then_inc(S["slots_t"], 1)

            def gates(n, i=0):
                pe.wait_ge(S["oh_ready"], i * 4 + (n + 1))
                wait(pe, S["g_taken"], i * 4 + (n - 1))
                for u in range(GTOK):
                    o = ps[:, 2 + n % 2, 2 * u * QKEYS:2 * (u + 1) * QKEYS]
                    pe.matmul(o.rearrange("p (q e) -> p q e", q=2), OHB[:, n % 2, :, u], OHA[:, n % 2, 0:2, :, u],
                              start=True, stop=False, skip_group_check=True)
                    ins = pe.matmul(o[:, QKEYS:], OHB[:, n % 2, :, u], OHA[:, n % 2, 2, :, u],
                                    start=False, stop=True, skip_group_check=True)
                ins.then_inc(S["oh_used"], 1)

            def first_quarter(n0):
                for g in range(4):
                    gates(n0 + g)
                with pe.Fori(1, GROUPS // 4) as i:
                    for g in range(4):
                        gates(n0 + g, i)

            def experts(p):
                n0, k0, m0, g0 = AT_PEER[p], p * N_PEER, p * NKEY, PASS_GROUP[p]

                def first_half(m, slot, i=0):
                    k = tile_u(m)
                    pe.wait_ge(S["w_used"], i * TURN + (n0 + k + 1))
                    wait(pe, S["gelu_done"], i * 4 + (m0 + m - 1))
                    r = k % 4
                    group(ps[:, slot % 2, 0:SEQ],
                          [x for c in range(KD) for x in parts(WHI[:, r, c, :], WLO[:, r, c, :], XHI[:, c, :], XLO[:, c, :])],
                          "part_used")

                def second_half(m, i=0):
                    k = tile_v(m)
                    pe.wait_ge(S["w_used"], i * TURN + (n0 + k + 1))
                    pe.wait_ge(S["act_ready"], i * 4 + (m0 + m + 1))
                    begin, end = (isinstance(i, int) and m == x for x in (0, NKEY - 1))
                    r, b = k % 4, m % 2
                    for c in range(KD):
                        out_c = ps[:, 4 + c // 2, c % 2 * SEQ:(c % 2 + 1) * SEQ]
                        for n, (w, x) in enumerate(parts(WHI[:, r, c, :], WLO[:, r, c, :], ACH[:, b, :], ACL[:, b, :])):
                            ins = pe.matmul(out_c, w, x, start=begin and c % 2 == 0 and n == 0, stop=end and n == 2,
                                            skip_group_check=True)
                    ins.then_inc(S["part_used"], 1)

                def turn(q, i, e0):
                    for e in range(e0, e0 + 4):
                        if e + 1 < NKEY:
                            first_half(e + 1, e + 1, i)
                        if p == 0 or q < QUARTERS - 1:
                            gates(g0 + e, i)
                        if p == 1 and isinstance(i, int) and e == 0:
                            pe.wait_ge(S["h_ready"], 2 * KD)
                        second_half(e, i)

                pe.wait_ge(S["x_ready"], KD * (p + 1))
                first_half(0, 0)
                turn(0, 0, 0)
                if p == 0:
                    with pe.Fori(1, NKEY // 4 - 1) as i:
                        turn(0, i, 0)
                else:
                    with pe.Fori(1, 3 * QKEYS // 4) as i:
                        turn(0, i, 0)
                    with pe.Fori(0, QKEYS // 4 - 1) as i:
                        turn(3, i, 3 * QKEYS)
                turn(3, 0, NKEY - 4)

            def hg_in():
                for j in range(N_HGIN):
                    n = AT_HGIN + j
                    wait(pe, S["hg_taken"], j - 3)
                    o = ps[:, j % 4, :]
                    if j < HG_SPLIT:
                        width = T if j >= 8 else SEQ
                        product("hg", j, o[:, 0:width], width)
                        continue
                    landed(pe, n)
                    if j < 32:
                        for t in range(TT):
                            ins = group(o[:, t * P:(t + 1) * P],
                                        [(A[:, k, t * P:(t + 1) * P], W[:, n % RING, k, :]) for k in range(KD)])
                        ins.then_inc(S["w_used"], 1)
                    else:
                        group(o[:, 0:SEQ], [(W[:, n % RING, k, :], A[:, k, 0:SEQ]) for k in range(KD)], "w_used")

            def states():
                pe.wait_ge(S["hg_taken"], N_HGIN)
                pe.wait_ge(S["ck_ready"], 3)
                for n in range(8):
                    t, d, hh = n // 4, n // 2 % 2, n % 2
                    wait(pe, S["ck_in"], n - 3)
                    for h in range(4):
                        ins = pe.transpose(ps[:, n % 4, h * P:(h + 1) * P], CK[:, d, 4 * hh + h, t * P:(t + 1) * P],
                                           ident[:, :])
                    ins.then_inc(S["ck_t"], 1)
                pe.wait_ge(S["ck_in"], 8)
                for n in range(4):
                    d, hh = n // 2, n % 2
                    for h in range(4):
                        hd = 4 * hh + h
                        ins = group(ps[:, 4 + n, h * P:(h + 1) * P],
                                    [(CKT[:, t, d, hd, :], IV[:, 2 + t, hd, :]) for t in range(2)])
                    ins.then_inc(S["cs_ready"], 1)
                pe.wait_ge(S["lk_ready"], 2)
                for n in range(4):
                    d, hh = n // 2, n % 2
                    for h in range(4):
                        ins = pe.transpose(ps[:, n, h * P:(h + 1) * P], LK[:, d, 4 * hh + h, :], ident[:, :])
                    ins.then_inc(S["lk_t"], 1)
                pe.wait_ge(S["cs_taken"], 4)
                pe.wait_ge(S["lk_in"], 4)
                for n in range(4):
                    d, hh = n // 2, n % 2
                    for h in range(4):
                        hd = 4 * hh + h
                        ins = group(ps[:, 4 + n, h * P:(h + 1) * P], [(LKT[:, d, hd, :], IV[:, d, hd, :])])
                    ins.then_inc(S["ls_ready"], 1)

            def levels():
                for lv in range(LEVELS + 1):
                    pe.wait_ge(S["lv_ready"], lv + 1)
                    q, k = LV[lv % 2]
                    for b in range(4):
                        wait(pe, S["lv_taken"], 4 * (lv - 1) + b + 1)
                        for m in range(4):
                            ins = pe.matmul(ps[:, b, m * P:(m + 1) * P], k[:, 4 * b + m, :], q[:, 4 * b + m, :],
                                            start=True, stop=True)
                        ins.then_inc(S["lv_prod"], 1)
                pe.wait_ge(S["lv_taken"], 4 * (LEVELS + 1))
                pe.wait_ge(S["ls_done"], 4)
                pe.wait_ge(S["qi_ready"], 2)
                for h in range(NH):
                    for t in range(2):
                        cols = slice(h % 2 * SEQ + t * P, h % 2 * SEQ + (t + 1) * P)
                        ins = group(ps[:, 4 + h // 2, cols],
                                    [(ST[:, t, 0, h, :], QI[:, 0, h, t * P:(t + 1) * P]),
                                     (ST[:, 1 - t, 1, h, :], QI[:, 1, h, t * P:(t + 1) * P]),
                                     (IV[:, t, h, :], AT_[:, 2 * h + t, :])])
                    if h % 2:
                        ins.then_inc(S["oi_ready"], 1)
                for b in range(4):
                    pe.wait_ge(S["osq_ready"], b + 1)
                    pe.matmul(ps[:, b, :], ones[:, :], OSQ[:, 2 * b:2 * b + 2, :].rearrange("p h t -> p (h t)"),
                              start=True, stop=True).then_inc(S["ors_ready"], 1)

            ada(0)
            ada(1)
            filters()
            pe.wait_ge(S["f_spectaken"], 8)
            norm(0, T)
            ab_in()
            hyena()
            rope()
            attention()
            pe.wait_ge(S["att_done"], 4)
            mixer_out(0, AT_ABOUT, MIX, T)
            norm(1, T)
            queries(0, T)
            routing(0, TT)
            first_quarter(0)
            experts(0)
            experts(1)
            norm(2, T)
            hg_in()
            states()
            levels()
            pe.wait_ge(S["mx_ready"], 4)
            mixer_out(1, AT_HGOUT, MX1, SEQ)
            norm(3, SEQ)
            queries(1, SEQ)
            routing(1, CHUNKS)
            first_quarter(2 * QUARTERS * GROUPS)
            experts(2)
            norm(4, SEQ)

        @block.scalar
        def _(act):
            for dst, src in filters_in:
                act.dma_start(dst, src).then_inc(S["f_in"], 16)
            for dst, src in arena_loads:
                act.dma_start(dst, src).then_inc(S["arena_in"], 16)
            copy = nc.scalar.copy

            act.wait_ge(S["c_in"], 16)
            act.activation(csil[:, :], csil[:, :], ACT.Silu).then_inc(S["c_ready"], 1)

            def filters():
                for n in range(2):
                    act.wait_ge(S["f_arg"], n + 1)
                    act.activation(FHID[n], FARG, ACT.Sin).then_inc(S["f_sin"], 1)
                for t in range(2):
                    act.wait_ge(S["f_rawtaken"], 4 * (t + 1))
                    act.activation(HABS[:, t].rearrange("p o d c -> p (o d c)"),
                                   HRAW[:, t].rearrange("p o d c -> p (o d c)"), ACT.Abs).then_inc(S["f_abs"], 1)

            def norm(k, width, streams):
                for c in range(KD):
                    act.activation(SQ[:, c, 0:width], H[:, c, 0:width], ACT.Square).then_inc(S["sq_ready"], 1)
                act.wait_ge(S["ms_ready"], k + 1)
                act.activation(rstd[:, 0:width], rstd[:, 0:width], ACT.Sqrt).then_inc(S["std_ready"], 1)
                if k < 4:
                    act.wait_ge(S["mods_ready"], k + 1)
                for c in range(KD):
                    act.wait_ge(S["hn_ready"], KD * k + c + 1)
                    for s in range(streams):
                        cols = slice(s * SEQ, (s + 1) * SEQ)
                        if k < 4:
                            ins = act.activation(A[:, c, cols], SQ[:, c, cols], ACT.Identity,
                                                 scale=GM[:, k, c, s:s + 1], bias=M[:, k // 2, k % 2 * 3, c, s:s + 1])
                        else:
                            ins = act.activation(A[:, c, cols], SQ[:, c, cols], ACT.Identity, scale=GN[:, 4, c:c + 1])
                    ins.then_inc(S["a_ready"], 1)
                    if 1 <= k < 4:
                        act.wait_ge(S["a_ready"], KD * k + c + 1)
                        copy(A_HI[:, c, 0:width], A[:, c, 0:width]).then_inc(S["a_hi_ready"], 1)

            def weight_high(name, j):
                n0, count, m0, _, _, ring, (w_hi, _), _ = SPLIT[name]
                if j < count:
                    landed(act, n0 + j)
                    wait(act, S["product_ready"], m0 + j - ring + 1 if j >= ring else 0)
                    copy(w_hi[:, j % ring], W[:, (n0 + j) % RING]).then_inc(S["w_hi_ready"], 1)

            def first_weights(name):
                for j in range(SPLIT[name][5] - 1):
                    weight_high(name, j)

            def ab_in():
                for j in range(N_ABIN):
                    act.wait_ge(S["w_used"], at_abin(j) + 1)
                    dst = U[:, j, :] if j < 12 else QT[:, j - 12, :] if j < 16 else KT if j == 16 else \
                        VT.rearrange("p t n -> p (t n)")
                    copy(dst, ps[:, j % 4, :]).then_inc(S["ab_taken"], 1)
                    c = j - 1
                    if 0 <= c < 12:
                        act.wait_ge(S["ab_taken"], c + 1)
                        act.activation(UC[:, c, :], U[:, c, :], ACT.Identity, scale=conv[:, 12 + c:13 + c],
                                       bias=conv[:, 36 + c:37 + c]).then_inc(S["cv_mid"], 1)

            def hyena():
                for o in range(2):
                    for t in range(TT):
                        act.wait_ge(S["zt_ready"], TT * o + t + 1)
                        copy(ZT[:, t, :], ps[:, t, :]).then_inc(S["zt_taken"], 1)

            def attention():
                def exps(u):
                    c, g, i = u // 8, u // 4 % 2, u % 4
                    h = 4 * g + c
                    n = 512 if i < 2 else 256
                    act.wait_ge(S["nmax_ready"], u + 1)
                    wait(act, S["pt_ready"], u - 1)
                    r = 4 * (u % 2)
                    act.activation(APR[:, u % 2, 0:n], ASC[:, u % 2, 0:n], ACT.Exp, bias=small[:, r:r + 1],
                                   scale=HD ** -0.5, accum_out=small[:, r + 1:r + 2])
                    act.activation(small[:, r + 2:r + 3], sinks[:, h:h + 1], ACT.Exp, bias=small[:, r:r + 1])\
                        .then_inc(S["exp_ready"], 1)

                def turned(u):
                    i = u % 4
                    n = 512 if i < 2 else 256
                    act.wait_ge(S["pt_ready"], u + 1)
                    wait(act, S["pv_done"], u - 1)
                    copy(APT[:, u % 2].rearrange("p k q -> p (k q)")[:, 0:n], ps[:, 2 + u % 2, 0:n])\
                        .then_inc(S["pt_taken"], 1)

                for u in range(35):
                    if u < 32:
                        exps(u)
                    if 1 <= u < 33:
                        turned(u - 1)
                    if u >= 3 and (u - 3) % 8 == 7:
                        c = (u - 3) // 8
                        act.wait_ge(S["pv_done"], 8 * (c + 1))
                        copy(MIX[:, 4 + c, :], ps[:, 4 + c % 2, :]).then_inc(S["att_done"], 1)

            def queries(l, width):
                _, _, m0, _, _, ring, _, _ = SPLIT[f"wq{l}"]
                for j in range(N_WQ):
                    weight_high(f"wq{l}", j + ring - 1)
                    act.wait_ge(S["product_ready"], m0 + j + 1)
                    copy(PQT[:, j, 0:width], ps[:, j % 4, 0:width]).then_inc(S["wq_taken"], 1)

            def routing(l, tiles):
                base = (0, TT)[l]
                act.wait_ge(S["wq_taken"], N_WQ * (l + 1))

                def queries_in(i):
                    copy(PQC, PQT[:, :, bass.ds(i * P, P)]).then_inc(S["qc_ready"], 1)
                    act.wait_ge(S["route_scores"], i + (base + 1))
                    wait(act, S["scores_used"], i + base)
                    copy(PS1.rearrange("p (b j) n -> p b (j n)", b=4), ps[:, 0:4, :]).then_inc(S["scores_ready"], 1)

                def exps(i):
                    act.wait_ge(S["diff_ready"], i + (base + 1))
                    act.activation(GATE[:, 0, :, :], GATE[:, 0, :, :], ACT.Exp).then_inc(S["gate_exp"], 1)

                def turned(i):
                    act.wait_ge(S["slots_t"], i + (base + 1))
                    copy(SL[:, :, bass.ds(i * P, P)], ps[:, 4, 0:3 * P].rearrange("p (q t) -> p q t", q=3))\
                        .then_inc(S["slots_in"], 1)

                queries_in(0)
                with act.Fori(0, tiles - 1) as i:
                    exps(i)
                    queries_in(i + 1)
                    turned(i)
                exps(tiles - 1)
                turned(tiles - 1)

            def gates_high(n, buf, g, i=0):
                act.wait_ge(S["oh_used"], i * 4 + (n + 1))
                copy(G[:, buf, :, bass.ds(i * 4 * GTOK + g * GTOK, GTOK)], gate_sums(n)[:, 0]).then_inc(S["g_high"], 1)

            def first_quarter(n0):
                for g in range(4):
                    gates_high(n0 + g, 0, g)
                with act.Fori(1, GROUPS // 4) as i:
                    for g in range(4):
                        gates_high(n0 + g, 0, g, i)

            def high(p, k, i=0):
                n = AT_PEER[p] + k
                landed(act, n, i)
                wait(act, S["part_used"], i * TURN + (p * N_PEER + k - 3))
                copy(WHI[:, k % 4].rearrange("p k n -> p (k n)"), wring[:, n % RING * TILE:(n % RING + 1) * TILE])\
                    .then_inc(S["hi_ready"], 1)

            def tokens(p):
                wait(act, S["part_used"], p * N_PEER)
                t0 = PASS_TOK[p]
                for c in range(KD):
                    copy(XHI[:, c, :], A[:, c, t0:t0 + SEQ]).then_inc(S["xhi_ready"], 1)

            def first_tiles(p):
                for k in range(3):
                    high(p, k)

            def experts(p):
                k0, m0, g0 = p * N_PEER, p * NKEY, PASS_GROUP[p]

                def turn(q, i, e0):
                    for m in range(e0, e0 + 4):
                        act.wait_ge(S["part_used"], i * TURN + (k0 + tile_u(m) + 1) if isinstance(i, int) or m else
                                    i * TURN + k0)
                        wait(act, S["act_ready"], i * 4 + (m0 + m - 1))
                        act.activation(GL[:, m % 2, :], ps[:, m % 2, 0:SEQ], ACT.Gelu).then_inc(S["gelu_done"], 1)
                        if m + 2 < NKEY:
                            high(p, tile_u(m + 2), i)
                        act.wait_ge(S["mul_ready"], i * 4 + (m0 + m + 1))
                        copy(ACH[:, m % 2, :], GL[:, m % 2, :]).then_inc(S["acthi_ready"], 1)
                        if m + 1 < NKEY:
                            high(p, tile_v(m + 1), i)
                        if p == 0 or q < QUARTERS - 1:
                            gates_high(g0 + m, (q + 1) % 2, m % QKEYS, i)

                quarters(act, turn)

            def hg_in():
                for j in range(N_HGIN):
                    if j == 26:
                        act.wait_ge(S["fk_done"], 16)
                        act.activation(LF.rearrange("p m t -> p (m t)"), LF.rearrange("p m t -> p (m t)"), ACT.Ln)\
                            .then_inc(S["ln_done"], 1)
                    if j == 35:
                        context_decays()
                    if j < HG_SPLIT:
                        _, _, m0, _, _, ring, _, _ = SPLIT["hg"]
                        weight_high("hg", j + ring - 1)
                        act.wait_ge(S["product_ready"], m0 + j + 1)
                    else:
                        act.wait_ge(S["w_used"], AT_HGIN + j + 1)
                    src = ps[:, j % 4, :]
                    if j < 8:
                        ins = act.activation(RQ[:, j, :], src[:, 0:SEQ], ACT.Silu)
                    elif j < 24:
                        ins = act.activation(LF[:, j - 8, :], src, ACT.Sigmoid)
                    elif j < 32:
                        ins = copy(IV[:, :, j - 24, :], src.rearrange("p (t n) -> p t n", t=TT))
                    else:
                        ins = act.activation(RG[:, j - 32, :], src[:, 0:SEQ], ACT.Silu)
                    ins.then_inc(S["hg_taken"], 1)

            def context_decays():
                act.wait_ge(S["scan_done"], 1)
                for h in range(NH):
                    act.activation(CK[:, 0, h, :], EC[:, 0, h, :], ACT.Exp, scale=-1.0, bias=EC[:, 0, h, SEQ - 1:SEQ])
                act.activation(CK[:, 1], EC[:, 1], ACT.Exp).then_inc(S["ck_exp"], 1)

            def states():
                for n in range(8):
                    t, d, hh = n // 4, n // 2 % 2, n % 2
                    act.wait_ge(S["ck_t"], n + 1)
                    copy(CKT[:, t, d, 4 * hh:4 * hh + 4, :].rearrange("p h n -> p (h n)"), ps[:, n % 4, :])\
                        .then_inc(S["ck_in"], 1)
                act.wait_ge(S["ck_t"], 8)
                for h in range(NH):
                    act.activation(LK[:, 0, h, :], EL[:, 0, 2 * h, 1:129], ACT.Exp, scale=-1.0,
                                   bias=EL[:, 0, 2 * h, 128:129])
                    ins = act.activation(LK[:, 1, h, :], EL[:, 1, 2 * h + 1, 0:128], ACT.Exp)
                ins.then_inc(S["lk_exp"], 1)
                for h in range(NH):
                    for t in range(2):
                        m = 2 * h + t
                        act.activation(QI[:, 0, h, t * P:(t + 1) * P], EL[:, 0, m, 1:129], ACT.Exp)
                        ins = act.activation(QI[:, 1, h, t * P:(t + 1) * P], EL[:, 1, m, 0:128], ACT.Exp, scale=-1.0,
                                             bias=EL[:, 1, m, 128:129])
                ins.then_inc(S["qi_exp"], 1)
                for n in range(4):
                    d, hh = n // 2, n % 2
                    act.wait_ge(S["cs_ready"], n + 1)
                    copy(ST[:, 0, d, 4 * hh:4 * hh + 4, :].rearrange("p h n -> p (h n)"), ps[:, 4 + n, :])\
                        .then_inc(S["cs_taken"], 1)
                act.wait_ge(S["dec_in"], 1)
                act.activation(lbs[:, 16:32], lbs[:, 0:16], ACT.Exp).then_inc(S["dec_exp"], 1)
                act.wait_ge(S["cs_ready"], 4)
                for n in range(4):
                    d, hh = n // 2, n % 2
                    act.wait_ge(S["lk_t"], n + 1)
                    copy(LKT[:, d, 4 * hh:4 * hh + 4, :].rearrange("p h n -> p (h n)"), ps[:, n, :])\
                        .then_inc(S["lk_in"], 1)

            def levels():
                for lv in range(LEVELS):
                    for n, b in enumerate(LV[lv % 2]):
                        act.wait_ge(S["lv_diff"], 2 * lv + n + 1)
                        act.activation(b, b, ACT.Exp).then_inc(S["lv_exp"], 1)
                for b in range(4):
                    act.wait_ge(S["oi_ready"], b + 1)
                    act.activation(OSQ[:, 2 * b:2 * b + 2, :].rearrange("p h t -> p (h t)"), ps[:, 4 + b, :], ACT.Square)\
                        .then_inc(S["osq_ready"], 1)
                act.wait_ge(S["oms_ready"], 4)
                act.activation(ORS, ORS, ACT.Sqrt).then_inc(S["ostd_ready"], 1)

            act.wait_ge(S["consts_in"], 16 * len(first))
            act.wait_ge(S["lb_diff"], 2)
            act.activation(lbs[:, 32:64], lbs[:, 32:64], ACT.Exp).then_inc(S["lb_exp"], 1)
            filters()
            act.wait_ge(S["x_in"], 16)
            norm(0, T, 2)
            ab_in()
            hyena()
            attention()
            act.wait_ge(S["h_ready"], KD)
            first_weights("wq0")
            norm(1, T, 2)
            queries(0, T)
            tokens(0)
            routing(0, TT)
            first_tiles(0)
            first_quarter(0)
            experts(0)
            tokens(1)
            first_tiles(1)
            experts(1)
            act.wait_ge(S["h_ready"], 3 * KD)
            first_weights("hg")
            norm(2, T, 2)
            hg_in()
            states()
            levels()
            act.wait_ge(S["h_ready"], 4 * KD)
            first_weights("wq1")
            norm(3, SEQ, 1)
            queries(1, SEQ)
            tokens(2)
            routing(1, CHUNKS)
            first_tiles(2)
            first_quarter(2 * QUARTERS * GROUPS)
            experts(2)
            act.wait_ge(S["h_ready"], 5 * KD)
            norm(4, SEQ, 1)

        @block.vector
        def _(dve):
            step = Chain(dve, S["dve_step"], settle_dve)
            tt, ts, stt = dve.tensor_tensor, dve.tensor_scalar, dve.scalar_tensor_tensor

            def bounds():
                l0, l1 = lbs[:, 0:16], lbs[:, 16:32]
                step.done(tt(lbs[:, 64:80], l0, l1, ALU.max))
                for n in range(2):
                    tt(lbs[:, 32 + 16 * n:48 + 16 * n], lbs[:, 16 * n:16 * n + 16], lbs[:, 64:80], ALU.subtract)\
                        .then_inc(S["lb_diff"], 1)
                dve.wait_ge(S["lb_exp"], 1)
                step.done(tt(lbs[:, 80:96], lbs[:, 32:48], lbs[:, 48:64], ALU.add))
                step.done(dve.reciprocal(lbs[:, 80:96], lbs[:, 80:96]))
                for n in range(2):
                    step.done(tt(lbs[:, 32 + 16 * n:48 + 16 * n], lbs[:, 32 + 16 * n:48 + 16 * n], lbs[:, 80:96],
                                 ALU.mult))
                step.done(tt(lbs[:, 96:112], lbs[:, 32:48], lbs[:, 48:64], ALU.add))
                step.done(tt(lbs[:, 96:112], lbs[:, 96:112], lbs[:, 32:48], ALU.subtract))
                step.done(ts(lbs[:, 112:128], lbs[:, 96:112], -1.0, 1.0, ALU.mult, ALU.add))

            def filters():
                dve.wait_ge(S["f_in"], 16 * len(filters_in))
                for n in range(2):
                    dve.wait_ge(S["f_proj"], n + 1)
                    step.done(ts(FARG, ps[0:64, n, 0:256], filt[0:64, n:n + 1], filt[0:64, 2:3], ALU.add, ALU.mult))
                    step.done(ts(FRND, FARG, 1.0 / TWO_PI, ROUND, ALU.mult, ALU.add))
                    step.done(ts(FRND, FRND, ROUND, None, ALU.subtract))
                    for part in (PI_A, PI_B, PI_C):
                        step.done(stt(FARG, FRND, -part, FARG, ALU.mult, ALU.add))
                    ts(FARG, FARG, 3.1415925, -3.1415925, ALU.min, ALU.max).then_inc(S["f_arg"], 1)
                ada(2)
                ada(3)
                for n in range(8):
                    t, od = n // 4, n % 4
                    dve.wait_ge(S["f_raw"], n + 1)
                    tt(HRAW[:, t, od // 2, od % 2, :], ps[:, 2 + n % 2, :], DECAY[:, t, :], ALU.mult)\
                        .then_inc(S["f_rawtaken"], 1)
                dve.wait_ge(S["f_abs"], 2)
                dve.wait_ge(S["f_rawtaken"], 8)
                for o in range(2):
                    step.done(dve.memset(HRAW[0:1, 0, o, 1, :], 0.0))
                for o in range(2):
                    for t in range(2):
                        tt(HSUM[:, o, t, :], HRAW[:, t, o, 0, :], HRAW[:, t, o, 1, :], ALU.add)
                        ins = tt(HDIF[:, o, t, :], HRAW[:, t, o, 0, :], HRAW[:, t, o, 1, :], ALU.subtract)
                ins.then_inc(S["f_parts"], 1)
                for o in range(2):
                    dve.wait_ge(S["f_norm"], o + 1)
                    step.done(dve.reciprocal(RNRM[:, o, :], ps[:, 4 + o, :]))
                for n in range(8):
                    o, q, f = n // 4, n // 2 % 2, n % 2
                    dve.wait_ge(S["f_spec"], n + 1)
                    tt(HF[:, o, q, f, :], ps[:, 6 + n % 2, :], RNRM[:, o, :], ALU.mult).then_inc(S["f_spectaken"], 1)

            def ada(g):
                m, count, pos = ADA_GROUPS[g]
                dve.wait_ge(S["w_used"], pos + count)
                tt(M2[:, m:m + count, :], ps[:, 5 + g % 2, 0:2 * count].rearrange("p (m z) -> p m z", z=2),
                   adab[:, m:m + count].unsqueeze(2).to_broadcast([P, count, 2]), ALU.add).then_inc(S["ada_taken"], 1)

            def gains_of(norms, groups):
                dve.wait_ge(S["ada_taken"], groups)
                for n in norms:
                    stt(GM[:, n], M[:, n // 2, n % 2 * 3 + 1], 1.0, GN[:, n, :].unsqueeze(2).to_broadcast([P, KD, 2]),
                        ALU.add, ALU.mult).then_inc(S["mods_ready"], 1)

            def norm(k, width):
                dve.wait_ge(S["norm_summed"], k + 1)
                ts(rstd[:, 0:width], ps[:, 7, 0:width], 1.0 / D, EPS, ALU.mult, ALU.add).then_inc(S["ms_ready"], 1)
                dve.wait_ge(S["std_ready"], k + 1)
                step.done(dve.reciprocal(rstd[:, 0:width], rstd[:, 0:width]))
                for c in range(KD):
                    tt(SQ[:, c, 0:width], H[:, c, 0:width], rstd[:, 0:width], ALU.mult).then_inc(S["hn_ready"], 1)

            def weight_low(name, j):
                n0, count, m0, _, _, ring, (w_hi, w_lo), _ = SPLIT[name]
                if j < count:
                    dve.wait_ge(S["w_hi_ready"], m0 + j + 1)
                    tt(w_lo[:, j % ring], W[:, (n0 + j) % RING], w_hi[:, j % ring], ALU.subtract)\
                        .then_inc(S["w_used"], 1)

            def first_parts(name):
                _, _, _, k, width, ring, _, a_lo = SPLIT[name]
                for j in range(ring - 1):
                    weight_low(name, j)
                for c in range(KD):
                    dve.wait_ge(S["a_hi_ready"], KD * (k - 1) + c + 1)
                    tt(a_lo[:, c, 0:width], A[:, c, 0:width], A_HI[:, c, 0:width], ALU.subtract)\
                        .then_inc(S["a_parts_ready"], 1)

            def query_weights(l):
                first_parts(f"wq{l}")
                for j in range(SPLIT[f"wq{l}"][5] - 1, N_WQ):
                    weight_low(f"wq{l}", j)

            def short_conv():
                ucs = UC.rearrange("p j (s t) -> p j s t", s=2)
                us = U.rearrange("p j (s t) -> p j s t", s=2)
                for j in range(12):
                    dve.wait_ge(S["cv_mid"], j + 1)
                    stt(ucs[:, j, :, 1:SEQ], us[:, j, :, 0:SEQ - 1], conv[:, j:j + 1], ucs[:, j, :, 1:SEQ],
                        ALU.mult, ALU.add).then_inc(S["dve_step"], 1)
                step.n += 12
                dve.wait_ge(S["dve_step"], step.n)
                for j in range(12):
                    ins = stt(ucs[:, j, :, 0:SEQ - 1], us[:, j, :, 1:SEQ], conv[:, 24 + j:25 + j],
                              ucs[:, j, :, 0:SEQ - 1], ALU.mult, ALU.add)
                ins.then_inc(S["cv_done"], 1)
                dve.wait_ge(S["cv_done"], 1)

            def hyena():
                for o in range(2):
                    z = UC if o == 0 else Z1
                    for n in range(4):
                        s, f = n // 2, n % 2
                        dve.wait_ge(S["zf_ready"], 4 * o + n + 1)
                        if o == 1 and n == 0:
                            dve.wait_ge(S["yt_ready"], HC)
                        zc, zs = ps[:, 4 + 2 * (n % 2), :], ps[:, 5 + 2 * (n % 2), :]
                        hc, hs = HF[:, o, 0, f, :], HF[:, o, 1, f, :]
                        t0, t1 = RTMP[:, 0:512], hand[:, 512:1024]
                        tt(PF[:, s, 0, f, :], zc, hc, ALU.mult)
                        tt(PF[:, s, 1, f, :], zc, hs, ALU.mult)
                        tt(t0, zs, hs, ALU.mult)
                        step.done(tt(t1, zs, hc, ALU.mult))
                        tt(PF[:, s, 0, f, :], PF[:, s, 0, f, :], t0, ALU.subtract)
                        ins = tt(PF[:, s, 1, f, :], PF[:, s, 1, f, :], t1, ALU.add)
                        ins.then_inc(S["pf_ready"], 1)
                        dve.wait_ge(S["pf_ready"], 4 * o + n + 1)
                    for c in range(HC):
                        dve.wait_ge(S["yt_ready"], HC * o + c + 1)
                        dst = Z1[:, c, :] if o == 0 else MIX[:, c, :]
                        step.done(stt(RTMP, z[:, c, :], dskip[:, HC * o + c:HC * o + c + 1], ps[:, c, :],
                                      ALU.mult, ALU.add))
                        tt(dst, RTMP, UC[:, 4 * (o + 1) + c, :], ALU.mult).then_inc(S["z_ready"], 1)
                        dve.wait_ge(S["z_ready"], HC * o + c + 1)

            def rope():
                dve.wait_ge(S["arena_in"], 32)
                for j in range(5):
                    x = QT[:, j, 0:SEQ] if j < 4 else KT[:, 0:SEQ]
                    dve.wait_ge(S["rot_ready"], j + 1)
                    step.done(tt(RTMP[:, 0:SEQ], ps[:, 4 + j % 2, 0:SEQ], ROPE[:, 1, :], ALU.mult))
                    step.done(tt(x, x, ROPE[:, 0, :], ALU.mult))
                    tt(x, x, RTMP[:, 0:SEQ], ALU.add).then_inc(S["rope_done"], 1)
                    dve.wait_ge(S["rope_done"], j + 1)

            def attention():
                step.done(ts(sinks[:, NQ:2 * NQ], sinks[:, 0:NQ], -1.0, None, ALU.mult))

                def maxima(u):
                    c, g, i = u // 8, u // 4 % 2, u % 4
                    h = 4 * g + c
                    n = 512 if i < 2 else 256
                    r = 4 * (u % 2)
                    dve.wait_ge(S["sc_ready"], u + 1)
                    wait(dve, S["exp_ready"], u - 1)
                    if i < 2:
                        ins = tt(ASC[:, u % 2, 0:n], ps[:, u % 2, 0:n], AMASK[:, i, :], ALU.add)
                    else:
                        ins = dve.tensor_copy(ASC[:, u % 2, 0:n], ps[:, u % 2, 0:n])
                    ins.then_inc(S["sc_taken"], 1)
                    dve.wait_ge(S["sc_taken"], u + 1)
                    step.done(dve.tensor_reduce(small[:, r + 3:r + 4], ASC[:, u % 2, 0:n], AXX, ALU.max, negate=True))
                    ts(small[:, r:r + 1], small[:, r + 3:r + 4], HD ** -0.5, sinks[:, NQ + h:NQ + h + 1],
                       ALU.mult, ALU.min).then_inc(S["nmax_ready"], 1)

                def normalise(u):
                    i = u % 4
                    n = 512 if i < 2 else 256
                    r = 4 * (u % 2)
                    dve.wait_ge(S["exp_ready"], u + 1)
                    step.done(tt(small[:, r + 2:r + 3], small[:, r + 1:r + 2], small[:, r + 2:r + 3], ALU.add))
                    step.done(dve.reciprocal(small[:, r + 2:r + 3], small[:, r + 2:r + 3]))
                    ts(APR[:, u % 2, 0:n], APR[:, u % 2, 0:n], small[:, r + 2:r + 3], None, ALU.mult)\
                        .then_inc(S["pn_ready"], 1)

                for u in range(33):
                    if u < 32:
                        maxima(u)
                    if u >= 1:
                        normalise(u - 1)

            def residual(l, kind, n0, bank, width, streams, ready):
                for c in range(KD):
                    ready(c)
                    for s in streams:
                        cols = slice(s * SEQ, (s + 1) * SEQ)
                        ins = stt(H[:, c, cols], bank(c, s), M[:, l, kind, c, s:s + 1], H[:, c, cols], ALU.mult, ALU.add)
                    ins.then_inc(S["h_ready"], 1)

            def routing(l, tiles):
                base = (0, TT)[l]
                n0 = step.n

                def wide(t, shape):
                    return t.to_broadcast(shape)

                def top(count, vals, vals2, tops, idx):
                    for j in range(count):
                        ins = dve.max(tops[:, j, 0:8], vals[:, j, :])
                    step.done(ins)
                    for j in range(count):
                        dve.max_index(idx[:, j, 0:8], tops[:, j, 0:8], vals[:, j, :])
                        ins = dve.match_replace(vals2[:, j, :], tops[:, j, 0:8], vals[:, j, :], NEG)
                    step.done(ins)
                    for j in range(count):
                        ins = dve.max(tops[:, j, 8:16], vals2[:, j, :])
                    step.done(ins)
                    for j in range(count):
                        ins = dve.max_index(idx[:, j, 8:16], tops[:, j, 8:16], vals2[:, j, :])
                    step.done(ins)

                with dve.Fori(0, tiles) as i:
                    step.enter(i, ROUTE_STEPS)
                    dve.wait_ge(S["scores_ready"], i + (base + 1))
                    settle_dve()
                    top(16, PS1, PS2, TV, TIU)
                    dve.tensor_copy(TIF, TIU).then_inc(S["scores_used"], 1)
                    tv = TV.rearrange("p (h q) k -> p h q k", q=2)
                    step.done(tt(CAND.rearrange("p h (i j) -> p h i j", i=TOPK),
                                 wide(tv[:, :, 0, :].unsqueeze(3), [P, NH, TOPK, TOPK]),
                                 wide(tv[:, :, 1, :].unsqueeze(2), [P, NH, TOPK, TOPK]), ALU.add))
                    top(NH, CAND, CAN2, SV, SJU)
                    tt(GATE[:, 0], SV, wide(SV[:, :, 0:1], [P, NH, TOPK]), ALU.subtract).then_inc(S["diff_ready"], 1)
                    ts(HIU[:, 0], SJU, 4, None, ALU.logical_shift_right)
                    step.done(ts(HIU[:, 1], SJU, 15, None, ALU.bitwise_and))
                    step.done(dve.tensor_copy(HIF, HIU))
                    tif = TIF.rearrange("p (h q) k -> p h q k", q=2)
                    for q in range(2):
                        i16 = I16.unsqueeze(1).to_broadcast([P, NH * TOPK, TOPK])
                        hf = HIF[:, q].rearrange("p h k -> p (h k)").unsqueeze(2)
                        step.done(tt(EQ.rearrange("p h k m -> p (h k) m"), i16, wide(hf, [P, NH * TOPK, TOPK]),
                                     ALU.is_equal))
                        step.done(tt(EQ, EQ, wide(tif[:, :, q, :].unsqueeze(2), [P, NH, TOPK, TOPK]), ALU.mult))
                        step.done(dve.tensor_reduce(GATE[:, 1 + q], EQ, AXX, ALU.add))
                    dve.wait_ge(S["gate_exp"], i + (base + 1))
                    step.done(dve.tensor_reduce(GSUM[:, 0], GATE[:, 0], AXX, ALU.add))
                    step.done(dve.reciprocal(GSUM[:, 1], GSUM[:, 0]))
                    tt(GATE[:, 0], GATE[:, 0], wide(GSUM[:, 1].unsqueeze(2), [P, NH, TOPK]), ALU.mult)\
                        .then_inc(S["gates_ready"], 1)
                    if l == 0:
                        m, count, pos = ADA_GROUPS[ROUTE_GROUP]
                        dve.wait_ge(S["w_used"], i * count + (pos + count))
                        mm = bass.ds(i * count + m, count)
                        tt(M2[:, mm, :], ps[:, 5, 0:2 * count].rearrange("p (m z) -> p m z", z=2),
                           adab[:, mm].unsqueeze(2).to_broadcast([P, count, 2]), ALU.add).then_inc(S["ada_taken"], 1)
                    dve.wait_ge(S["slots_t"], i + (base + 1))
                step.leave(tiles, n0)

            def onehots(n, quarter, t0, g, i=0):
                toks = bass.ds(i * 4 * GTOK + (t0 + g * GTOK), GTOK)
                wait(dve, S["oh_used"], i * 4 + (n - 1))
                wait(dve, S["oh_ready"], i * 4 + (n - 1))
                wide = [P, QKEYS, GTOK]
                tt(EQK[:, n % 2], KEYNUM[:, quarter * QKEYS:(quarter + 1) * QKEYS, :],
                   KEY12[:, 0, toks].unsqueeze(1).to_broadcast(wide), ALU.is_equal).then_inc(S["eq_ready"], 1)
                tt(OHB[:, n % 2], KEYNUM, KEY12[:, 1, toks].unsqueeze(1).to_broadcast([P, P, GTOK]), ALU.is_equal)
                dve.wait_ge(S["eq_ready"], i * 4 + (n + 1))
                parts = [P, 3, QKEYS, GTOK]
                tt(OHA[:, n % 2], EQK[:, n % 2].unsqueeze(1).to_broadcast(parts),
                   GP[:, :, toks].unsqueeze(2).to_broadcast(parts), ALU.mult).then_inc(S["oh_ready"], 1)

            def gates_in(n, buf, g, i=0):
                dve.wait_ge(S["g_high"], i * 4 + (n + 1))
                x = G[:, buf, :, bass.ds(i * 4 * GTOK + g * GTOK, GTOK)]
                tt(x, x, gate_sums(n)[:, 1], ALU.add).then_inc(S["g_taken"], 1)

            def first_quarter(n0, tiles, width):
                dve.wait_ge(S["slots_in"], tiles)
                wait(dve, S["oh_used"], n0)
                rest, last = GREST[:, 0:width], SL[:, 0, 0:width]
                for part in range(3):
                    step.done(dve.tensor_copy(GP[:, part, 0:width], last))
                    if part < 2:
                        step.done(tt(rest, last, GP[:, part, 0:width], ALU.subtract))
                        last = rest
                dve.tensor_copy(KEYNUM, iota[:, :].unsqueeze(2).to_broadcast([P, P, GTOK]))
                step.done(dve.tensor_copy(KEY12[:, :, 0:width], SL[:, 1:3, 0:width]))
                for g in range(4):
                    onehots(n0 + g, 0, 0, g)
                    if g:
                        gates_in(n0 + g - 1, 0, g - 1)
                with dve.Fori(1, GROUPS // 4) as i:
                    for g in range(4):
                        onehots(n0 + g, 0, 0, g, i)
                        gates_in(n0 + g - 1, 0, g - 1, i)
                gates_in(n0 + GROUPS - 1, 0, GROUPS - 1)

            def low(p, k, i=0):
                n = AT_PEER[p] + k
                dve.wait_ge(S["hi_ready"], i * TURN + (p * N_PEER + k + 1))
                tt(WLO[:, k % 4].rearrange("p k n -> p (k n)"), wring[:, n % RING * TILE:(n % RING + 1) * TILE],
                   WHI[:, k % 4].rearrange("p k n -> p (k n)"), ALU.subtract).then_inc(S["w_used"], 1)

            def tokens(p):
                t0 = PASS_TOK[p]
                for c in range(KD):
                    dve.wait_ge(S["xhi_ready"], KD * p + c + 1)
                    tt(XLO[:, c, :], A[:, c, t0:t0 + SEQ], XHI[:, c, :], ALU.subtract).then_inc(S["x_ready"], 1)

            def first_tiles(p):
                for k in range(3):
                    low(p, k)

            def experts(p):
                m0, g0 = p * NKEY, PASS_GROUP[p]

                def turn(q, i, e0):
                    for m in range(e0, e0 + 4):
                        if p == 0 or q < QUARTERS - 1:
                            nq = (q + 1) % QUARTERS
                            onehots(g0 + m, nq, SEQ if p == 1 or nq == 0 else 0, m % QKEYS, i)
                        dve.wait_ge(S["gelu_done"], i * 4 + (m0 + m + 1))
                        tt(GL[:, m % 2, :], GL[:, m % 2, :],
                           G[:, q % 2, bass.ds(i * 4 + m % QKEYS, 1), :].rearrange("p e t -> p (e t)"), ALU.mult)\
                            .then_inc(S["mul_ready"], 1)
                        if m + 2 < NKEY:
                            low(p, tile_u(m + 2), i)
                        dve.wait_ge(S["acthi_ready"], i * 4 + (m0 + m + 1))
                        tt(ACL[:, m % 2, :], GL[:, m % 2, :], ACH[:, m % 2, :], ALU.subtract)\
                            .then_inc(S["act_ready"], 1)
                        if m + 1 < NKEY:
                            low(p, tile_v(m + 1), i)
                        if p == 0 or q < QUARTERS - 1:
                            gates_in(g0 + m, (q + 1) % 2, m % QKEYS, i)

                quarters(dve, turn, lambda q: dve.wait_ge(S["g_taken"], g0 + q * QKEYS))

            def peer_residual(p, l, s):
                def ready(c):
                    if c == 0:
                        dve.wait_ge(S["part_used"], (p + 1) * N_PEER)
                residual(l, 5, 0, lambda c, _: ps[:, 4 + c // 2, c % 2 * SEQ:(c % 2 + 1) * SEQ], SEQ, [s], ready)

            def forget():
                first_parts("hg")
                for j in range(1, 9):
                    weight_low("hg", j)
                for m in range(16):
                    weight_low("hg", m + 9)
                    dve.wait_ge(S["hg_taken"], 8 + m + 1)
                    step.done(ts(LF[:, m, :], LF[:, m, :], lbs[:, 112 + m:113 + m], lbs[:, 96 + m:97 + m],
                                 ALU.mult, ALU.add))
                    d, h = m // 8, m % 8
                    ts(RKL[:, d, h, :], LF[:, m, 0:SEQ], -1.0, 1.0, ALU.mult, ALU.add)
                    ts(RKC[:, d, h, :], LF[:, m, SEQ:T], -1.0, 1.0, ALU.mult, ALU.add).then_inc(S["fk_done"], 1)
                dve.wait_ge(S["ln_done"], 1)
                dve.wait_ge(S["a_ready"], 3 * KD)
                one = hand[:, 0:SEQ]
                dve.memset(EL[:, :, :, 0:1], 0.0)
                dve.memset(EC[:, 1, :, 0:1], 0.0)
                step.done(dve.memset(one, 1.0))
                for h in range(NH):
                    dve.tensor_tensor_scan(EC[:, 0, h, :], one, LF[:, h, SEQ:T], 0.0, ALU.mult, ALU.add)
                    dve.tensor_tensor_scan(EC[:, 1, h, 1:SEQ], one[:, 0:SEQ - 1], LF[:, 8 + h, SEQ:T - 1], 0.0,
                                           ALU.mult, ALU.add)
                for m in range(16):
                    for d in range(2):
                        ins = dve.tensor_tensor_scan(EL[:, d, m, 1:129], one[:, 0:P],
                                                     LF[:, 8 * d + m // 2, m % 2 * P:(m % 2 + 1) * P], 0.0,
                                                     ALU.mult, ALU.add)
                ins.then_inc(S["scan_done"], 1)

            def states():
                dve.wait_ge(S["ck_exp"], 1)
                tt(CK[:, 0], CK[:, 0], RKC[:, 0], ALU.mult).then_inc(S["ck_ready"], 1)
                tt(CK[:, 1], CK[:, 1], RKC[:, 1], ALU.mult).then_inc(S["ck_ready"], 2)
                dve.wait_ge(S["lk_exp"], 1)
                tt(LK[:, 0], LK[:, 0], RKL[:, 0, :, 0:P], ALU.mult).then_inc(S["lk_ready"], 1)
                tt(LK[:, 1], LK[:, 1], RKL[:, 1, :, P:SEQ], ALU.mult).then_inc(S["lk_ready"], 1)
                dve.wait_ge(S["qi_exp"], 1)
                for d in range(2):
                    tt(QI[:, d], QI[:, d], RQ, ALU.mult).then_inc(S["qi_ready"], 1)
                dve.tensor_copy(lbs[:, 0:8], EL[:, 0, 0:16:2, 128])
                dve.tensor_copy(lbs[:, 8:16], EL[:, 1, 1:16:2, 128]).then_inc(S["dec_in"], 1)

            def carry():
                dve.wait_ge(S["dec_exp"], 1)
                for n in range(4):
                    d, hh = n // 2, n % 2
                    dve.wait_ge(S["ls_ready"], n + 1)
                    for h in range(4):
                        hd = 4 * hh + h
                        ins = stt(ST[:, 1, d, hd, :], ST[:, 0, d, hd, :], lbs[:, 16 + 8 * d + hd:17 + 8 * d + hd],
                                  ps[:, 4 + n, h * P:(h + 1) * P], ALU.mult, ALU.add)
                    ins.then_inc(S["ls_done"], 1)

            def levels():
                def split(lv, x):
                    m = P >> (lv + 1)
                    return m, x.rearrange("p m (s u) -> p m s u", s=P // (2 * m))

                def half(lv, x, lo):
                    m, y = split(lv, x)
                    return y[:, :, :, lo * m:lo * m + m]

                def differences(lv):
                    q, k = LV[lv % 2]
                    if lv >= 2:
                        dve.wait_ge(S["lv_prod"], 4 * (lv - 1))

                    def cut(x, off, lo):
                        return half(lv, x[:, :, off:off + P], lo)

                    def mid(x):
                        m, y = split(lv, x[:, :, 0:P])
                        return y[:, :, :, m:m + 1].to_broadcast([P, 16, P // (2 * m), m])

                    ef, eb = EL[:, 0], EL[:, 1]
                    tt(half(lv, q, 1), cut(ef, 1, 1), mid(ef), ALU.subtract)
                    tt(half(lv, q, 0), mid(eb), cut(eb, 0, 0), ALU.subtract).then_inc(S["lv_diff"], 1)
                    tt(half(lv, k, 0), mid(ef), cut(ef, 1, 0), ALU.subtract)
                    tt(half(lv, k, 1), cut(eb, 0, 1), mid(eb), ALU.subtract).then_inc(S["lv_diff"], 1)

                def operands_of(lv):
                    q, k = LV[lv % 2]
                    qv = q.rearrange("p (h t) n -> p h (t n)", h=NH)
                    if lv == LEVELS:
                        kv = k.rearrange("p (h t) n -> p h (t n)", h=NH)
                        dve.wait_ge(S["lv_prod"], 4 * (lv - 1))
                        dve.tensor_copy(qv, RQ)
                        tt(kv, RKL[:, 0], RKL[:, 1], ALU.add).then_inc(S["lv_ready"], 1)
                        return
                    dve.wait_ge(S["lv_exp"], 2 * lv + 1)
                    tt(qv, qv, RQ, ALU.mult)
                    dve.wait_ge(S["lv_exp"], 2 * lv + 2)
                    kl = RKL.rearrange("p d h (t n) -> p d (h t) n", t=2)
                    tt(half(lv, k, 0), half(lv, k, 0), half(lv, kl[:, 0], 0), ALU.mult)
                    tt(half(lv, k, 1), half(lv, k, 1), half(lv, kl[:, 1], 1), ALU.mult).then_inc(S["lv_ready"], 1)

                def place(lv):
                    for b in range(4):
                        dve.wait_ge(S["lv_prod"], 4 * lv + b + 1)
                        dve.copy_predicated(AT_[:, 4 * b:4 * b + 4, :],
                                            masks[:, lv, :].unsqueeze(1).to_broadcast([P, 4, P]),
                                            ps[:, b, :].rearrange("p (m t) -> p m t", m=4)).then_inc(S["lv_taken"], 1)

                dve.wait_ge(S["masks_in"], 16)
                dve.wait_ge(S["ls_ready"], 4)
                differences(0)
                operands_of(0)
                for lv in range(LEVELS + 1):
                    if lv + 1 < LEVELS:
                        differences(lv + 1)
                    place(lv)
                    if lv + 1 <= LEVELS:
                        operands_of(lv + 1)

            def readout():
                for b in range(4):
                    dve.wait_ge(S["ors_ready"], b + 1)
                    ts(ORS[:, 2 * b:2 * b + 2, :].rearrange("p h t -> p (h t)"), ps[:, b, :], 1.0 / P, EPS,
                       ALU.mult, ALU.add).then_inc(S["oms_ready"], 1)
                dve.wait_ge(S["ostd_ready"], 1)
                step.done(dve.reciprocal(ORS, ORS))
                for b in range(4):
                    o = ORS[:, 2 * b:2 * b + 2, :]
                    step.done(tt(o, ps[:, 4 + b, :].rearrange("p (h t) -> p h t", h=2), o, ALU.mult))
                    stt(MX1[:, 2 * b:2 * b + 2, :], o, ong[:, 0:1], RG[:, 2 * b:2 * b + 2, :], ALU.mult, ALU.mult)\
                        .then_inc(S["mx_ready"], 1)

            dve.wait_ge(S["consts_in"], 16 * len(first))
            bounds()
            ada(0)
            ada(1)
            filters()
            gains_of([0], 4)
            norm(0, T)
            for g in range(FIRST_GROUPS, ROUTE_GROUP):
                ada(g)
            gains_of([1], ROUTE_GROUP)
            short_conv()
            hyena()
            rope()
            attention()
            residual(0, 2, 0, lambda c, s: ps[:, c % 4, s * SEQ:(s + 1) * SEQ], T, [0, 1],
                     lambda c: dve.wait_ge(S["w_used"], AT_ABOUT + c + 1))
            norm(1, T)
            query_weights(0)
            tokens(0)
            routing(0, TT)
            gains_of([2, 3], ROUTE_GROUP + TT)
            first_tiles(0)
            first_quarter(0, TT, T)
            experts(0)
            peer_residual(0, 0, 0)
            tokens(1)
            first_tiles(1)
            experts(1)
            peer_residual(1, 0, 1)
            norm(2, T)
            forget()
            states()
            carry()
            levels()
            readout()
            residual(1, 2, 0, lambda c, s: ps[:, c % 4, 0:SEQ], SEQ, [0],
                     lambda c: dve.wait_ge(S["w_used"], AT_HGOUT + c + 1))
            norm(3, SEQ)
            query_weights(1)
            tokens(2)
            routing(1, CHUNKS)
            first_tiles(2)
            first_quarter(2 * QUARTERS * GROUPS, TT + CHUNKS, SEQ)
            experts(2)
            peer_residual(2, 1, 0)
            norm(4, SEQ)


def tables():
    f32 = np.float32
    t = {"ident": np.eye(P, dtype=f32), "ones": np.ones((P, P), f32),
         "iota": np.tile(np.arange(P, dtype=f32), (P, 1))}
    f, n = np.arange(256)[:, None], np.arange(256)[None, :]
    ang = np.pi * (2 * f + 1) * n / 512.0
    cut = lambda m: m.reshape(2, P, 256).transpose(1, 0, 2).reshape(P, 512)
    t["dft"] = np.concatenate([cut(np.cos(ang).T), cut(np.sin(ang).T), cut(np.cos(ang) / 256), cut(np.sin(ang) / 256)],
                              axis=1).astype(f32)
    lin = np.linspace(0.0, 1.0, SEQ, dtype=f32)[:, None]
    w = (f32(2.0 * np.pi) * np.arange(SEQ, dtype=f32)[:, None] / f32(SEQ)).astype(f32)
    fr = np.linspace(1e-4, 15, 16, dtype=f32)[None, :]
    fw = (fr * w).astype(f32)
    t["zpos"] = np.concatenate([lin, np.cos(fw), -np.sin(fw)], axis=1).T.astype(f32)
    deltas = np.abs(np.linspace(np.log(1e-2) / 1.5, np.log(1e-2) / 0.3, HYC, dtype=f32))
    t["decay"] = np.exp(-lin * deltas).astype(f32).reshape(2, P, HYC).transpose(1, 0, 2).reshape(P, 1024)
    am = np.zeros((P, 2, 512), f32)
    q, k = np.arange(P)[:, None], np.arange(256)[None, :]
    for i in range(2):
        am[:, i, 0:256] = np.where(np.abs(q + i * P - k) <= 128, 0.0, -1.0e30)
    t["amask"] = am.reshape(P, 1024)
    inv = (10000.0 ** (-np.arange(16, dtype=f32) / 16)).astype(f32)
    pos = [np.repeat(np.arange(SEQ // 64), 64).astype(f32), np.tile(np.arange(64), SEQ // 64).astype(f32)]
    rope = np.zeros((P, 640), f32)
    for p in range(P):
        d = p % 64
        x = (pos[d // 32] * inv[d % 16]).astype(f32)
        rope[p, 0:256], rope[p, 256:512] = np.cos(x), np.sin(x)
        b = d % 32 >= 16
        rope[p - 16 if b else p + 16, 512 + p] = 1.0 if b else -1.0
    t["rope"] = rope
    s, u = np.arange(P)[:, None], np.arange(P)[None, :]
    m = [((s >> (6 - lv)) ^ (u >> (6 - lv))) == 1 for lv in range(7)] + [s == u]
    t["masks"] = np.concatenate(m, axis=1).astype(f32)
    return t


def tiles(w):
    n = w.shape[1]
    return np.ascontiguousarray(w.reshape(KD, P, n // P, P).transpose(2, 1, 0, 3)).reshape(n // P, P, TILE)


def columns(v):
    return np.asarray(v).reshape(-1, P).T


def layout(x, c, ctx, c_ctx, ada_w, ada_b, norm1_g, norm2_g, final_g, ab_w_in, ab_w_out,
           hy_conv_w, hy_conv_b, hy_filt_w1, hy_filt_b1, hy_filt_w2, hy_filt_b2, hy_filt_w3,
           hy_filt_freq, hy_skip, attn_sink, hg_w_in, hg_w_out, hg_lb_logits, hg_onorm_g,
           peer_wq, peer_keys, peer_u, peer_v):
    a = tables()
    xt = np.concatenate([x[0], ctx[0]], axis=0).T
    a["xT"] = xt.reshape(KD, P, T).transpose(1, 0, 2).reshape(P, KD * T)
    a["cc"] = np.stack([columns(c[0]), columns(c_ctx)], axis=2).reshape(P, 2 * KD)
    a["ada"] = np.concatenate([tiles(ada_w[l]) for l in range(2)])
    a["adab"] = np.concatenate([columns(ada_b[l]) for l in range(2)], axis=1)
    a["gains"] = np.concatenate([columns(g) for g in (norm1_g[0], norm2_g[0], norm1_g[1], norm2_g[1], final_g)], axis=1)
    order = np.concatenate([np.arange(h * HD, (h + 1) * HD) for c in range(4) for h in (c, c + 4)])
    win = np.concatenate([ab_w_in[0][:, :1536], ab_w_in[0][:, 1536 + order], ab_w_in[0][:, 2048:]], axis=1)
    a["abin"] = tiles(win)
    a["about"] = tiles(np.concatenate([ab_w_out[0][:512], ab_w_out[0][512 + order]], axis=0))
    a["conv"] = np.concatenate([columns(hy_conv_w[0][n]) for n in range(3)] + [columns(hy_conv_b[0])], axis=1)
    a["dskip"] = np.concatenate([columns(hy_skip[0][n]) for n in range(2)], axis=1)
    a["sink"] = np.tile(attn_sink[0][None, :], (P, 1))
    a["fw1"], a["fw2"], a["fw3"] = hy_filt_w1[0], hy_filt_w2[0], hy_filt_w3[0]
    a["fvec"] = np.stack([hy_filt_b1[0], hy_filt_b2[0], hy_filt_freq[0]], axis=1)
    a["lbl"] = np.concatenate([columns(hg_lb_logits[n].reshape(-1)) for n in range(2)], axis=1)
    a["ong"] = hg_onorm_g[0][:, None]
    a["hgin"], a["hgout"] = tiles(hg_w_in[0]), tiles(hg_w_out[0])
    for l in range(2):
        a[f"wq{l}"] = tiles(peer_wq[l])
        a[f"keys{l}"] = peer_keys[l].reshape(16, NKEY, P).transpose(2, 0, 1).reshape(P, 16 * NKEY)
        a[f"u{l}"] = np.ascontiguousarray(peer_u[l].reshape(NKEY, NKEY, KD, P).transpose(0, 3, 2, 1))\
            .reshape(NKEY, P, TILE)
        a[f"v{l}"] = peer_v[l].reshape(NKEY, NKEY, D)
    return {k: np.ascontiguousarray(v) for k, v in a.items()}


def kernel(**inputs):
    import concourse.bacc as bacc
    from concourse.bass_utils import run_bass_kernel_spmd

    arrays = layout(**{k: np.asarray(v) for k, v in inputs.items()})
    nc = bacc.Bacc("TRN2", target_bir_lowering=False, num_devices=1)
    aps = {k: nc.dram_tensor(f"in_{k}", v.shape, mybir.dt.from_np(v.dtype), kind="ExternalInput").ap()
           for k, v in arrays.items()}
    out = nc.dram_tensor("out_t", (P, KD, SEQ), F32, kind="ExternalOutput").ap()
    build(nc, aps, out)
    r = run_bass_kernel_spmd(nc, [{f"in_{k}": v for k, v in arrays.items()}], core_ids=[0])
    got = np.asarray(r.results[0]["out_t"]).reshape(P, KD, SEQ)
    return np.ascontiguousarray(got.transpose(2, 1, 0).reshape(1, SEQ, D))
```
